# Optimizing a Trainium2 kernel written in Bass

```python
import math
import jax, jax.numpy as jnp
from jax import lax
import numpy as np

D_MODEL = 1024
BATCH = 1
SEQ = 2048
DEPTH = 1

MEM_LEN = 256
EXPAND = 2
D_MIX = EXPAND * D_MODEL
D_CONV = 3 * D_MIX // 8
D_GMLP = 3 * D_MIX // 8
D_XATT = D_MIX - D_CONV - D_GMLP
N_XHEADS = 4
XHEAD_DIM = D_XATT // N_XHEADS
CONV_WIDTH = 31
N_CONV_GROUPS = D_CONV // 128
CHUNK = 128
GMLP_HEAD = 128
N_GMLP_HEADS = D_GMLP // GMLP_HEAD
ALPHA = (2.0 * DEPTH) ** 0.25
BETA = (8.0 * DEPTH) ** -0.25
LN_EPS = 1e-5
D_IN_PROJ = 3 * D_CONV + 3 * D_GMLP + 2 * D_XATT

kernel_name = "hybrid_conv_gmlp_memxattn_deepnorm"

def _layernorm(h, g, b):
    hf = h.astype(jnp.float32)
    mu = jnp.mean(hf, axis=-1, keepdims=True)
    var = jnp.mean(jnp.square(hf - mu), axis=-1, keepdims=True)
    return ((hf - mu) * lax.rsqrt(var + LN_EPS)).astype(h.dtype) * g + b

def _conv_branch(a, glu_g, conv_w, conv_b, ln_g, ln_b):
    h = a * jax.nn.sigmoid(glu_g)
    h = lax.conv_general_dilated(
        h, conv_w[:, None, :].astype(h.dtype), window_strides=(1,),
        padding=[(CONV_WIDTH - 1, 0)],
        dimension_numbers=("NWC", "WIO", "NWC"),
        feature_group_count=D_CONV) + conv_b
    h = _layernorm(h, ln_g, ln_b)
    return jax.nn.silu(h)

def _gmlp_branch(u, v, ln_g, ln_b, ws, bs):
    B, S, _ = u.shape
    v = _layernorm(v, ln_g, ln_b)
    v = v.reshape(B, S // CHUNK, CHUNK, N_GMLP_HEADS, GMLP_HEAD)
    causal = jnp.tril(jnp.ones((CHUNK, CHUNK), dtype=bool))
    ws_c = jnp.where(causal[None], ws, jnp.zeros((), ws.dtype))
    s = jnp.einsum("hts,bnshc->bnthc", ws_c, v) + jnp.transpose(bs)[None, None, :, :, None]
    return u * s.reshape(B, S, D_GMLP)

def _mem_xattn(q, mem, w_kv, b_kv):
    B, S, _ = q.shape
    kv = jnp.einsum("bmd,de->bme", mem, w_kv) + b_kv
    k, v = jnp.split(kv, 2, axis=-1)
    q = q.reshape(B, S, N_XHEADS, XHEAD_DIM)
    k = k.reshape(B, MEM_LEN, N_XHEADS, XHEAD_DIM)
    v = v.reshape(B, MEM_LEN, N_XHEADS, XHEAD_DIM)
    scores = jnp.einsum("bshd,bmhd->bhsm", q, k).astype(jnp.float32) * (XHEAD_DIM ** -0.5)
    p = jax.nn.softmax(scores, axis=-1).astype(v.dtype)
    o = jnp.einsum("bhsm,bmhd->bshd", p, v)
    return o.reshape(B, S, D_XATT)

def setup_inputs(seed: int = 0) -> dict:
    key = jax.random.key(seed)
    ks = jax.random.split(key, 20)
    f32 = jnp.float32
    L = DEPTH
    nrm = lambda k, shp: jax.random.normal(k, shp, f32)
    return {
        "x": nrm(ks[0], (BATCH, SEQ, D_MODEL)),
        "mem": nrm(ks[1], (BATCH, MEM_LEN, D_MODEL)),
        "w_in": nrm(ks[2], (L, D_MODEL, D_IN_PROJ)) * D_MODEL ** -0.5,
        "b_in": 0.02 * nrm(ks[3], (L, D_IN_PROJ)),
        "conv_w": nrm(ks[4], (L, CONV_WIDTH, D_CONV)) * CONV_WIDTH ** -0.5,
        "conv_b": 0.02 * nrm(ks[5], (L, D_CONV)),
        "conv_ln_g": 1.0 + 0.05 * nrm(ks[6], (L, D_CONV)),
        "conv_ln_b": 0.02 * nrm(ks[7], (L, D_CONV)),
        "gmlp_ln_g": 1.0 + 0.05 * nrm(ks[8], (L, D_GMLP)),
        "gmlp_ln_b": 0.02 * nrm(ks[9], (L, D_GMLP)),
        "gmlp_ws": nrm(ks[10], (L, N_GMLP_HEADS, CHUNK, CHUNK)) * CHUNK ** -0.5,
        "gmlp_bs": 1.0 + 0.05 * nrm(ks[11], (L, N_GMLP_HEADS, CHUNK)),
        "w_kv": nrm(ks[12], (L, D_MODEL, 2 * D_XATT)) * D_MODEL ** -0.5,
        "b_kv": 0.02 * nrm(ks[13], (L, 2 * D_XATT)),
        "w_out": nrm(ks[14], (L, D_MIX, D_MODEL)) * (D_MIX ** -0.5) * BETA,
        "b_out": 0.02 * nrm(ks[15], (L, D_MODEL)),
        "ln_g": 1.0 + 0.05 * nrm(ks[16], (L, D_MODEL)),
        "ln_b": 0.02 * nrm(ks[17], (L, D_MODEL)),
    }

def reference(x, mem, w_in, b_in, conv_w, conv_b, conv_ln_g, conv_ln_b, gmlp_ln_g, gmlp_ln_b,
              gmlp_ws, gmlp_bs, w_kv, b_kv, w_out, b_out, ln_g, ln_b):
    split_pts = np.cumsum([D_CONV, D_CONV, D_CONV, D_GMLP, D_GMLP, D_GMLP, D_XATT])
    for l in range(DEPTH):
        h = jnp.einsum("bsd,de->bse", x, w_in[l]) + b_in[l]
        (c_a, c_glu, c_gate, g_u, g_v, g_gate, xq, x_gate) = jnp.split(
            h, [int(p) for p in split_pts], axis=-1)
        y_conv = _conv_branch(c_a, c_glu, conv_w[l], conv_b[l], conv_ln_g[l], conv_ln_b[l])
        y_gmlp = _gmlp_branch(jax.nn.gelu(g_u), jax.nn.gelu(g_v), gmlp_ln_g[l], gmlp_ln_b[l],
                              gmlp_ws[l], gmlp_bs[l])
        y_xatt = _mem_xattn(xq, mem, w_kv[l], b_kv[l])
        y = jnp.concatenate([y_conv * jax.nn.silu(c_gate),
                             y_gmlp * jax.nn.silu(g_gate),
                             y_xatt * jax.nn.silu(x_gate)], axis=-1)
        y = jnp.einsum("bse,ed->bsd", y, w_out[l]) + b_out[l]
        x = _layernorm(ALPHA * x + y, ln_g[l], ln_b[l])
    return x


_drawn_inputs = setup_inputs


def setup_inputs(seed=0):
    import zlib

    import numpy as np

    out = dict(_drawn_inputs(seed))
    spreads = {}
    factors = {'mem': 3.901,
     'b_in': 8.0,
     'conv_b': 8.0,
     'conv_ln_g': 22.166,
     'conv_ln_b': 59.451,
     'gmlp_ln_g': 37.279,
     'gmlp_ln_b': 198.394,
     'gmlp_bs': 25.392,
     'w_kv': 3.712,
     'b_kv': 49.342,
     'b_out': 18.961,
     'ln_b': 2.881}
    for name, (base, spread) in spreads.items():
        noise = np.random.default_rng([zlib.crc32(name.encode()), seed]).standard_normal(out[name].shape)
        drawn = base * np.exp(spread * noise) if base else spread * noise
        out[name] = __import__('jax').numpy.asarray(drawn.astype(out[name].dtype))
    for name, factor in factors.items():
        out[name] = (out[name] * factor).astype(out[name].dtype)
    return out
```

```python
from contextlib import ExitStack

import concourse.bass as bass
from concourse import mybir

P = 128
F32 = mybir.dt.float32
F32R = mybir.dt.float32r
ACT = mybir.ActivationFunctionType
ALU = mybir.AluOpType
AX = mybir.AxisListType


class Signal:

    def __init__(self, sem, per, lead=0, unit=1):
        self.sem, self.per, self.lead, self.unit = sem, per, lead, unit

    def __call__(self, b, n):
        return self.sem, b * (self.per * self.unit) + (self.lead + n) * self.unit


def layer(nc, x, mem, w_in, b_in, conv_w, conv_b, conv_ln_g, conv_ln_b, gmlp_ln_g, gmlp_ln_b,
          gmlp_ws, gmlp_bs, w_kv, b_kv, w_out, b_out, ln_g, ln_b, out):
    _, S, D = x.shape
    MEM = mem.shape[1]
    E_IN = w_in.shape[2]
    TAPS = conv_w.shape[1]
    DC = conv_w.shape[2]
    E_OUT = w_out.shape[1]
    DX = w_kv.shape[2] // 2
    KD = D // P
    NG = DC // P
    NH = gmlp_ws.shape[1]
    NX = DX // P
    MC = MEM // P
    B = 512
    T = B // P
    BLOCKS = S // B
    HALF = 512
    NC_IN = E_IN // P
    NC_OUT = E_OUT // P
    CHUNKS = NC_IN + NC_OUT
    KV = 2 * NX
    WR = 3
    PAD = TAPS - 1
    ALPHA = 2.0 ** 0.25
    EPS = 1e-5
    SCALE = float(P) ** -0.5
    C2 = DC // 2
    assert NG == 6 and NH == 6 and NX == 4 and KD == 8 and T == 4 and MC == 2 and D == 2 * HALF
    assert CHUNKS % WR == 0 and BLOCKS * B == S and DX == HALF

    order = []
    others = ([("v", c) for c in range(6)] + [("gmlp_gate", c) for c in range(6)]
              + [("q", c) for c in range(4)] + [("x_gate", c) for c in range(2)])
    for g in range(NG):
        order += [("glu", g), ("a", g)] + others[3 * g:3 * g + 3]
    order += [("x_gate", 2), ("x_gate", 3)] + [("u", c) for c in range(6)]
    order += [("conv_gate", c) for c in range(6)]
    assert len(order) == NC_IN
    first = {"a": 0, "glu": 6, "conv_gate": 12, "u": 18, "v": 24, "gmlp_gate": 30, "q": 36,
             "x_gate": 40}
    step_of = {k: j for j, k in enumerate(order)}
    y_order = list(range(6, 16)) + list(range(6))
    side = {10: [("v_turn", 0), ("v_turn", 1)], 12: [("v_turn", 2), ("v_turn", 3)],
            15: [("mix", 0)], 18: [("mix", 1)], 20: [("mix", 2)],
            23: [("score", 0)], 24: [("score", 1)], 25: [("p_turn", 0)], 26: [("p_turn", 1)],
            27: [("score", 2)], 28: [("score", 3)], 29: [("attend", 0), ("attend", 1)],
            30: [("p_turn", 2)], 31: [("p_turn", 3)], 32: [("attend", 2)], 33: [("attend", 3)],
            34: [("c_turn", 0), ("c_turn", 1)], 36: [("c_turn", 2), ("c_turn", 3)],
            40: [("c_back", 0)], 42: [("c_back", 1)], 43: [("c_back", 2)]}
    PAIR_USES = [("x_turn", t) for t in range(T)]
    for j in range(NC_IN):
        PAIR_USES += side.get(j, [])
    PAIR_USES += [("out", 0), ("out", 1)]
    assert len(PAIR_USES) % 2 == 0
    use_of = {k: u for u, k in enumerate(PAIR_USES)}
    tmp_uses = []
    for j in range(NC_IN):
        if order[j][0] in ("glu", "u"):
            tmp_uses.append(order[j])
        for kind, i in side.get(j, []):
            if kind == "c_back":
                tmp_uses += [("silu", 2 * i), ("silu", 2 * i + 1)]
    tmp_of = {k: i for i, k in enumerate(tmp_uses)}
    gate_of = {k: i for i, k in enumerate([o for o in order if "gate" in o[0]])}
    N_TMP = len(tmp_uses)
    LN_V, LN_C, LN_O = 0, T, 2 * T
    N_LN = 3 * T
    TAP_OPS = TAPS + 1
    tap_plan = {}
    for g in range(NG):
        n = 0
        for s, k in enumerate([7, 7, 6, 6, 6]):
            tap_plan[5 * g + 2 + s] = [(g, n + i) for i in range(k)]
            n += k
        assert n == TAP_OPS

    ctx = ExitStack()
    with ctx:
        def sb(name, shape, dt=F32):
            return ctx.enter_context(nc.sbuf_tensor(name, shape, dt))

        def signal(name, per=0, lead=0, unit=1):
            return Signal(ctx.enter_context(nc.semaphore(name)), per, lead, unit)

        PS = ctx.enter_context(nc.psum_tensor("banks", [P, 8, HALF], F32))
        x_hi = sb("x_hi", [P, KD, B], F32R)
        x_lo = sb("x_lo", [P, KD, B], F32R)
        whl = sb("w_split", [P, WR, 2, KD * P], F32R)
        kt = sb("k_split", [P, 2, NX, MEM], F32R)
        vm = sb("v_split", [P, 2, MC, DX], F32R)
        wst = sb("ws_split", [P, 2, NH, P], F32R)
        side_r = sb("side_split", [P, 2 * T * DC], F32R)
        wstage = sb("w_stage", [P, WR, KD * P])
        work = sb("work", [P, T * D])
        res = sb("residual", [P, T, D])
        y = sb("y_t", [P, NC_OUT, B])
        gated = sb("gated", [P, 2, B])
        h = sb("conv_in", [P, 2, PAD + B])
        halo = sb("halo", [P, NG, PAD])
        even_sum = sb("even_sum", [P, B])
        ident = sb("ident", [P, P])
        mix_bias = sb("mix_bias", [P, NH, P])
        bout_bc = sb("b_out_rows", [P, D])
        lng_bc = sb("ln_g_rows", [P, D])
        lnb_bc = sb("ln_b_rows", [P, D])
        NV = NC_IN + KV + 5 * NG
        cols = sb("vector_columns", [P, NV])
        cw = sb("conv_w_columns", [P, NG, TAPS])
        neg_half = sb("neg_half", [P, 1])
        bn = sb("bn", [P, N_LN, 2, 6])
        mv = sb("mean_var", [P, N_LN, 2])
        ve = sb("var_eps", [P, N_LN])
        rstd = sb("rstd", [P, N_LN])
        mx = sb("score_max", [P, NX, T])
        nmx = sb("neg_max", [P, NX, T])
        sums = sb("exp_sums", [P, NX, T])
        inv = sb("inv_sums", [P, NX, T])

        yf = y[:].rearrange("p c s -> p (c s)")
        cw_nat = yf[0:TAPS, 0:DC]
        ws_nat = yf[:, DC:2 * DC].rearrange("p (h s) -> p h s", h=NH)
        ws_low = yf[:, 2 * DC:3 * DC].rearrange("p (h s) -> p h s", h=NH)
        bs_bc = yf[:, 3 * DC:4 * DC]
        vec_nat = yf[0:NV, 4 * DC:4 * DC + P]
        vt_nat = yf[:, 8 * HALF:8 * HALF + NX * MEM].rearrange("p (h m) -> p h m", h=NX)
        ones = side_r[:, 0:P]

        b_in_col = lambda c: cols[:, c:c + 1]
        b_kv_col = lambda c: cols[:, NC_IN + c:NC_IN + c + 1]
        vec_col = lambda k, c: cols[:, NC_IN + KV + k * NG + c:NC_IN + KV + k * NG + c + 1]
        CONV_B, CONV_G, CONV_BETA, GMLP_G, GMLP_BETA = range(5)

        def v_norm(part, t):
            return side_r[:, (part * T + t) * DC:(part * T + t + 1) * DC]

        def q_part(part, hd):
            return side_r[:, (hd % 2 * 2 + part) * B:(hd % 2 * 2 + part + 1) * B]

        def p_part(part, hd):
            at = 4 * B + (hd % 2 * 2 + part) * MC * B
            return side_r[:, at:at + MC * B].rearrange("p (c s) -> p c s", c=MC)

        def y_part(part, e):
            at = 8 * B + (e % 2 * 2 + part) * B
            return side_r[:, at:at + B]

        x_tile = lambda t: work[:, t * D:(t + 1) * D]
        v_act = lambda c: work[:, c * B:(c + 1) * B]
        v_tmp = work[:, NH * B:NH * B + DC]
        probs = lambda hd: work[:, hd % 2 * T * MEM:(hd % 2 + 1) * T * MEM].rearrange(
            "p (t m) -> p t m", t=T)
        c_norm = lambda t: work[:, t * DC:(t + 1) * DC]

        def pair_of(kind, i):
            p = use_of[(kind, i)] % 2
            return PS[:, 2 * p:2 * p + 2, :]

        def bank_of(j):
            return PS[:, 4 + j % 2, :]

        acc = [PS[:, 6, :], PS[:, 7, :]]

        mem_landed = signal("mem_landed")
        vec_landed = signal("vectors_landed")
        ws_landed = signal("ws_landed")
        rows_landed = signal("rows_landed")
        idr = signal("identity_ready")
        msk = signal("ws_masked")
        credit = signal("credits_given")
        vec_turned = signal("vectors_turned")
        vec_ready = signal("vectors_ready")
        mem_turned = signal("mem_turned")
        mem_hi = signal("mem_hi_ready")
        mem_split = signal("mem_split_ready")
        ws_turned = signal("ws_turned")
        ws_hi = signal("ws_hi_ready")
        ws_split = signal("ws_split_ready")
        row_sum = signal("ws_row_sums")
        bias_ready = signal("mix_bias_ready")
        kv_hi = signal("k_hi_or_v_ready")
        k_split = signal("k_split_ready")
        v_back = signal("v_memory_turned")
        v_hi = signal("v_memory_hi")
        v_split = signal("v_memory_split")

        w_landed = [signal(f"w_landed{s}", CHUNKS // WR, 0, 16) for s in range(WR)]
        w_hi = signal("w_hi_ready", CHUNKS, KV)
        w_split = signal("w_split_ready", CHUNKS, KV)
        chunk_done = signal("chunk_done", CHUNKS, KV)
        x_landed = [signal(f"x_landed{t}", 1, 0, 16) for t in range(T)]
        res_landed = [signal(f"residual_landed{t}", 1, 0, 16) for t in range(T)]
        stored = [signal(f"out_stored{t}", 1, 0, 16) for t in range(T)]
        x_turned = signal("x_turned", T)
        x_hi_ready = signal("x_hi_ready", T)
        x_split = signal("x_split_ready", T)
        tmp_full = signal("gated_full", N_TMP)
        tmp_used = signal("gated_used", N_TMP, 2)
        v_ready = signal("v_ready", NH)
        gate_ready = signal("gate_ready", len(gate_of))
        q_hi_ready = signal("q_hi_ready", NX)
        q_split = signal("q_split_ready", NX)
        halo_in = signal("halo_in", NG)
        halo_out = signal("halo_out", NG, NG)
        tap_done = signal("tap_done", NG * TAPS)
        conv_summed = signal("conv_summed", NG, 2)
        v_turned = signal("v_turned", T)
        v_normed = signal("v_normed", T)
        vn_hi = signal("v_norm_hi", T)
        vn_split = signal("v_norm_split", T)
        ln_stats = signal("ln_stats", 2 * N_LN)
        ln_mean = signal("ln_mean", N_LN)
        ln_var = signal("ln_var_eps", N_LN)
        ln_rstd = signal("ln_rstd", N_LN)
        mixed = signal("mixed", NH // 2)
        mix_scaled = signal("mix_scaled", NH)
        mix_gated = signal("mix_gated", NH)
        scored = signal("scored", NX)
        max_ready = signal("max_ready", NX)
        nmax_ready = signal("neg_max_ready", NX)
        exp_done = signal("exp_done", NX)
        inv_ready = signal("inv_ready", NX)
        p_ready = signal("probs_ready", NX)
        p_turned = signal("probs_turned", NX)
        p_hi_ready = signal("probs_hi_ready", NX)
        p_split = signal("probs_split_ready", NX)
        pv_done = signal("pv_done", NX)
        attended = signal("attended", NX)
        c_turned = signal("conv_turned", T)
        c_normed = signal("conv_normed", T)
        c_back = signal("conv_back", NG // 2)
        y_hi_ready = signal("y_hi_ready", NC_OUT)
        y_split = signal("y_split_ready", NC_OUT)
        out_ready = signal("out_ready", T - 1)
        res_scaled = signal("residual_scaled", T)
        res_summed = signal("residual_summed", T, T)
        ln_scaled = signal("out_ln_scaled", T)
        ln_done = signal("out_ln_done", T)

        def bank_released(b, j):
            kind, i = order[j]
            if kind in ("glu", "u"):
                return tmp_full(b, tmp_of[order[j]] + 1)
            if kind == "a":
                return tmp_used(b, tmp_of[("glu", i)] + 1)
            if kind == "v":
                return v_ready(b, i + 1)
            if kind == "q":
                return q_split(b, i + 1)
            return gate_ready(b, gate_of[order[j]] + 1)

        def pair_released(b, u):
            kind, i = PAIR_USES[u]
            return {
                "x_turn": lambda: x_split(b, i + 1),
                "v_turn": lambda: v_normed(b, i + 1),
                "mix": lambda: mix_gated(b, 2 * i + 2),
                "score": lambda: exp_done(b, i + 1),
                "p_turn": lambda: p_split(b, i + 1),
                "attend": lambda: attended(b, i + 1),
                "c_turn": lambda: c_normed(b, i + 1),
                "c_back": lambda: tmp_full(b, tmp_of[("silu", 2 * i + 1)] + 1),
                "out": lambda: res_summed(b, i + 1 - T),
            }[kind]()

        def y_final(b, c):
            if c < NG:
                return tmp_used(b, tmp_of[("silu", c)] + 1)
            if c < NG + NH:
                return tmp_used(b, tmp_of[("u", c - NG)] + 1)
            return attended(b, c - NG - NH + 1)

        slot_of = lambda j: (KV + j) % WR

        x_rows = x.rearrange("o s d -> (o s) d")
        out_rows = out.rearrange("o s d -> (o s) d")
        w_in_v = w_in.rearrange("l (k p) e -> p (l k) e", p=P)
        w_kv_v = w_kv.rearrange("l (k p) e -> p (l k) e", p=P)
        w_out_v = w_out.rearrange("l e n -> (l e) n")
        mem_rows = mem.rearrange("o m d -> (o m) d")

        block = ctx.enter_context(nc.Block())

        @block.sync
        def _(sp):
            def load_w(b, j):
                s = slot_of(j)
                if not (isinstance(b, int) and b == 0 and KV + j < WR):
                    sp.wait_ge(*w_split(b, j - WR + 1))
                dst = wstage[:, s, :]
                if j < 0:
                    src = w_kv_v[:, :, (KV + j) * P:(KV + j + 1) * P]
                elif j < NC_IN:
                    kind, i = order[j]
                    c = first[kind] + i
                    src = w_in_v[:, :, c * P:(c + 1) * P]
                else:
                    c = y_order[j - NC_IN]
                    sp.dma_start(dst, w_out_v[c * P:(c + 1) * P, :]).then_inc(w_landed[s].sem, 16)
                    return
                sp.dma_start(dst.rearrange("p (k e) -> p k e", k=KD), src).then_inc(w_landed[s].sem, 16)

            def load_x(b, t):
                sp.dma_start(x_tile(t), x_rows[bass.ds(b * B + t * P, P), :]).then_inc(x_landed[t].sem, 16)

            def load_rows(b, behind):
                for t in range(T):
                    if behind:
                        sp.wait_ge(*stored[t](b, 0))
                    sp.dma_start(res[:, t, :], x_rows[bass.ds(b * B + t * P, P), :]).then_inc(
                        res_landed[t].sem, 16)

            for i in range(MC):
                sp.dma_start(res[:, i, :], mem_rows[i * P:(i + 1) * P, :]).then_inc(mem_landed.sem, 16)
            load_w(0, -KV)
            load_w(0, 1 - KV)
            load_w(0, 2 - KV)
            for t in range(T):
                sp.dma_start(x_tile(t), x_rows[t * P:(t + 1) * P, :]).then_inc(x_landed[t].sem, 16)
            for j in range(WR - KV, 0):
                load_w(0, j)

            def sync_block(b, last):
                for j in range(CHUNKS):
                    load_w(b, j)
                    if j == 30 and last:
                        load_rows(b, True)
                    elif j == 30:
                        with sp.If(b > 0):
                            load_rows(b, True)
                        with sp.Else():
                            load_rows(b, False)
                    if j == NC_IN + 6 and not last:
                        sp.wait_ge(*c_back(b, NG // 2))
                        for t in range(T):
                            load_x(b + 1, t)

            sp.wait_ge(mem_turned.sem, MC)
            with sp.Fori(0, BLOCKS - 1) as b:
                sync_block(b, False)
            sync_block(BLOCKS - 1, True)
            for t in range(T):
                sp.wait_ge(*stored[t](BLOCKS - 1, 1))

        @block.tensor
        def _(pe):
            def turn_x(b):
                for t in range(T):
                    pe.wait_ge(*x_landed[t](b, 1))
                    u = use_of[("x_turn", t)]
                    pe.wait_ge(*(pair_released(b, u - 2)))
                    dst = pair_of("x_turn", t)
                    for k in range(KD):
                        m = pe.transpose(dst[:, k // 4, k % 4 * P:(k % 4 + 1) * P],
                                         x_tile(t)[:, k * P:(k + 1) * P], ident[:])
                    m.then_inc(x_turned.sem, 1)

            def product(dst, w, moving_hi, moving_lo, steps, n_inc):
                for k in range(steps):
                    pe.matmul(dst, w(0, k), moving_hi(k), start=(k == 0), stop=False)
                    pe.matmul(dst, w(0, k), moving_lo(k), start=False, stop=False)
                    m = pe.matmul(dst, w(1, k), moving_hi(k), start=False, stop=(k == steps - 1))
                if n_inc is not None:
                    m.then_inc(n_inc.sem, 1)

            def project(b, j):
                s = slot_of(j)
                pe.wait_ge(*w_split(b, j + 1))
                if j == 0:
                    pe.wait_ge(*x_split(b, T))
                if j < 2:
                    pe.wait_ge(*res_summed(b, 3 - T))
                else:
                    pe.wait_ge(*bank_released(b, j - 2))
                product(bank_of(j), lambda part, k: whl[:, s, part, k * P:(k + 1) * P],
                        lambda k: x_hi[:, k, :], lambda k: x_lo[:, k, :], KD, chunk_done)

            def side_stage(b, kind, i):
                pe.wait_ge(*pair_released(b, use_of[(kind, i)] - 2))
                dst = pair_of(kind, i)
                if kind == "v_turn":
                    pe.wait_ge(*v_ready(b, NH))
                    for c in range(NH):
                        m = pe.transpose(dst[:, c // 3, c % 3 * P:(c % 3 + 1) * P],
                                         v_act(c)[:, i * P:(i + 1) * P], ident[:])
                    m.then_inc(v_turned.sem, 1)
                elif kind == "mix":
                    pe.wait_ge(*vn_split(b, T))
                    for n, hd in enumerate((2 * i, 2 * i + 1)):
                        for t in range(T):
                            d = dst[:, n, t * P:(t + 1) * P]
                            vh = v_norm(0, t)[:, hd * P:(hd + 1) * P]
                            vl = v_norm(1, t)[:, hd * P:(hd + 1) * P]
                            pe.matmul(d, vh, wst[:, 0, hd, :], start=True, stop=False)
                            pe.matmul(d, vh, wst[:, 1, hd, :], start=False, stop=False)
                            m = pe.matmul(d, vl, wst[:, 0, hd, :], start=False, stop=True)
                    m.then_inc(mixed.sem, 1)
                elif kind == "score":
                    pe.wait_ge(*q_split(b, i + 1))
                    for t in range(T):
                        d = dst[:, t // 2, t % 2 * MEM:(t % 2 + 1) * MEM]
                        qh = q_part(0, i)[:, t * P:(t + 1) * P]
                        ql = q_part(1, i)[:, t * P:(t + 1) * P]
                        pe.matmul(d, qh, kt[:, 0, i, :], start=True, stop=False)
                        pe.matmul(d, qh, kt[:, 1, i, :], start=False, stop=False)
                        m = pe.matmul(d, ql, kt[:, 0, i, :], start=False, stop=True)
                    m.then_inc(scored.sem, 1)
                elif kind == "p_turn":
                    pe.wait_ge(*p_ready(b, i + 1))
                    for c in range(MC):
                        for t in range(T):
                            m = pe.transpose(dst[:, c, t * P:(t + 1) * P],
                                             probs(i)[:, t, c * P:(c + 1) * P], ident[:])
                    m.then_inc(p_turned.sem, 1)
                elif kind == "attend":
                    pe.wait_ge(*p_split(b, i + 1))
                    product(dst[:, 0, :], lambda part, k: vm[:, part, k, i * P:(i + 1) * P],
                            lambda k: p_part(0, i)[:, k, :], lambda k: p_part(1, i)[:, k, :],
                            MC, pv_done)
                elif kind == "c_turn":
                    pe.wait_ge(*conv_summed(b, NG))
                    for c in range(NG):
                        m = pe.transpose(dst[:, c // 3, c % 3 * P:(c % 3 + 1) * P],
                                         y[:, c, i * P:(i + 1) * P], ident[:])
                    m.then_inc(c_turned.sem, 1)
                elif kind == "c_back":
                    pe.wait_ge(*c_normed(b, T))
                    for n, c in enumerate((2 * i, 2 * i + 1)):
                        for t in range(T):
                            m = pe.transpose(dst[:, n, t * P:(t + 1) * P],
                                             c_norm(t)[:, c * P:(c + 1) * P], ident[:])
                    m.then_inc(c_back.sem, 1)

            def project_out(b, e):
                j = NC_IN + e
                s = slot_of(j)
                pe.wait_ge(*w_split(b, j + 1))
                pe.wait_ge(*y_split(b, e + 1))
                for t in range(T):
                    if e == 0:
                        if t < 2:
                            pe.wait_ge(*pair_released(b, use_of[("out", t)] - 2))
                        elif t == 2:
                            pe.wait_ge(*bank_released(b, NC_IN - 2))
                            pe.wait_ge(*bank_released(b, NC_IN - 1))
                        else:
                            pe.wait_ge(*conv_summed(b, NG))
                    yh = y_part(0, e)[:, t * P:(t + 1) * P]
                    yl = y_part(1, e)[:, t * P:(t + 1) * P]
                    wh = lambda n: whl[:, s, 0, n * HALF:(n + 1) * HALF]
                    wl = lambda n: whl[:, s, 1, n * HALF:(n + 1) * HALF]
                    d = lambda n: PS[:, 2 * t + n, :]
                    for n in range(2):
                        pe.matmul(d(n), yh, wh(n), start=(e == 0), stop=False)
                        pe.matmul(d(n), yh, wl(n), start=False, stop=False)
                    for n in range(2):
                        m = pe.matmul(d(n), yl, wh(n), start=False, stop=(e == NC_OUT - 1))
                    if e == NC_OUT - 1 and t < T - 1:
                        m.then_inc(out_ready.sem, 1)
                m.then_inc(chunk_done.sem, 1)

            pe.wait_ge(idr.sem, 2)
            pe.wait_ge(vec_landed.sem, 8 * 16)
            pe.transpose(PS[:, 4, 0:NV], vec_nat, ident[0:NV, 0:NV])
            for g in range(NG):
                m = pe.transpose(PS[:, 5, g * TAPS:(g + 1) * TAPS], cw_nat[:, g * P:(g + 1) * P],
                                 ident[0:TAPS, 0:TAPS])
            m.then_inc(vec_turned.sem, 1)
            pe.wait_ge(mem_landed.sem, MC * 16)
            for i in range(MC):
                for k in range(KD):
                    m = pe.transpose(PS[:, 2 * i + k // 4, k % 4 * P:(k % 4 + 1) * P],
                                     res[:, i, k * P:(k + 1) * P], ident[:])
                m.then_inc(mem_turned.sem, 1)
            pe.wait_ge(msk.sem, 1)
            for hd in range(NH):
                m = pe.transpose(PS[:, 6 + hd // 3, hd % 3 * P:(hd % 3 + 1) * P], ws_low[:, hd, :],
                                 ident[:])
            m.then_inc(ws_turned.sem, 1)
            pe.wait_ge(mem_split.sem, MC)
            pe.wait_ge(vec_ready.sem, 2)
            for c in range(KV):
                pe.wait_ge(*w_split(0, c - KV + 1))
                if c >= 2:
                    if c - 2 < NX:
                        pe.wait_ge(k_split.sem, c - 1)
                    else:
                        pe.wait_ge(kv_hi.sem, c - 1)
                s = c % WR
                product(PS[:, 4 + c % 2, 0:MEM], lambda part, k: whl[:, s, part, k * P:(k + 1) * P],
                        lambda k: x_hi[:, k, 0:MEM], lambda k: x_lo[:, k, 0:MEM], KD, chunk_done)
            pe.wait_ge(ws_split.sem, 1)
            for n in range(2):
                for part in range(2):
                    m = pe.matmul(PS[:, 6 + n, 0:C2], ones,
                                  wst[:, part, 3 * n:3 * n + 3, :], start=(part == 0), stop=(part == 1))
            m.then_inc(row_sum.sem, 1)
            pe.wait_ge(kv_hi.sem, KV)
            for c in range(MC):
                for hd in range(NX):
                    m = pe.transpose(PS[:, c, hd * P:(hd + 1) * P], vt_nat[:, hd, c * P:(c + 1) * P],
                                     ident[:])
            m.then_inc(v_back.sem, 1)
            pe.wait_ge(v_split.sem, 1)
            pe.wait_ge(bias_ready.sem, NH)
            pe.wait_ge(credit.sem, 1)

            def tensor_block(b, last):
                for j in range(NC_IN):
                    project(b, j)
                    for kind, i in side.get(j, []):
                        side_stage(b, kind, i)
                for e in range(NC_OUT):
                    project_out(b, e)
                if not last:
                    turn_x(b + 1)

            turn_x(0)
            with pe.Fori(0, BLOCKS - 1) as b:
                tensor_block(b, False)
            tensor_block(BLOCKS - 1, True)

        @block.scalar
        def _(act):
            def weight_hi(b, j):
                s = slot_of(j)
                n = (KV + j) // WR + 1
                act.wait_ge(w_landed[s].sem, b * (16 * (CHUNKS // WR)) + 16 * n)
                if not (isinstance(b, int) and b == 0 and KV + j < WR):
                    act.wait_ge(*chunk_done(b, j - WR + 1))
                act.copy(whl[:, s, 0, :], wstage[:, s, :]).then_inc(w_hi.sem, 1)

            def x_hi_tiles(b):
                for t in range(T):
                    act.wait_ge(*x_turned(b, t + 1))
                    act.copy(x_hi[:, :, t * P:(t + 1) * P],
                             pair_of("x_turn", t).rearrange("p a (k s) -> p (a k) s", s=P)).then_inc(
                        x_hi_ready.sem, 1)

            def from_bank(b, j):
                kind, i = order[j]
                src, bias = bank_of(j), b_in_col(first[kind] + i)
                if kind == "a":
                    return
                act.wait_ge(*chunk_done(b, j + 1))
                if kind in ("glu", "u"):
                    n = tmp_of[order[j]]
                    act.wait_ge(*tmp_used(b, n - 1))
                    act.activation(gated[:, n % 2, :], src,
                                   ACT.Sigmoid if kind == "glu" else ACT.Gelu_apprx_tanh,
                                   bias=bias).then_inc(tmp_full.sem, 1)
                elif kind == "v":
                    act.activation(v_act(i), src, ACT.Gelu_apprx_tanh, bias=bias).then_inc(v_ready.sem, 1)
                elif kind == "q":
                    act.activation(q_part(0, i), src, ACT.Identity, bias=bias).then_inc(q_hi_ready.sem, 1)
                else:
                    c = {"conv_gate": 0, "gmlp_gate": NG, "x_gate": NG + NH}[kind] + i
                    act.activation(y[:, c, :], src, ACT.Silu, bias=bias).then_inc(gate_ready.sem, 1)

            def side_stage(b, kind, i):
                if kind == "v_turn":
                    act.wait_ge(*v_normed(b, i + 1))
                    act.copy(v_norm(0, i), v_tmp).then_inc(vn_hi.sem, 1)
                elif kind == "score":
                    act.wait_ge(*scored(b, i + 1))
                    act.wait_ge(*nmax_ready(b, i + 1))
                    for t in range(T):
                        m = act.activation(probs(i)[:, t, :],
                                           pair_of(kind, i)[:, t // 2, t % 2 * MEM:(t % 2 + 1) * MEM],
                                           ACT.Exp, bias=nmx[:, i, t:t + 1], scale=SCALE,
                                           accum_out=sums[:, i, t:t + 1])
                    m.then_inc(exp_done.sem, 1)
                elif kind == "p_turn":
                    act.wait_ge(*p_turned(b, i + 1))
                    act.copy(p_part(0, i), pair_of(kind, i)).then_inc(p_hi_ready.sem, 1)
                elif kind == "c_back":
                    act.wait_ge(*c_back(b, i + 1))
                    for n, c in enumerate((2 * i, 2 * i + 1)):
                        k = tmp_of[("silu", c)]
                        act.wait_ge(*tmp_used(b, k - 1))
                        act.activation(gated[:, k % 2, :], pair_of(kind, i)[:, n, :], ACT.Silu,
                                       bias=vec_col(CONV_BETA, c), scale=vec_col(CONV_G, c)).then_inc(
                            tmp_full.sem, 1)

            def y_hi(b, e):
                if e >= 2:
                    act.wait_ge(*chunk_done(b, NC_IN + e - 1))
                act.wait_ge(*y_final(b, y_order[e]))
                act.copy(y_part(0, e), y[:, y_order[e], :]).then_inc(y_hi_ready.sem, 1)

            act.dma_start(vec_nat[0:NC_IN, :], b_in.rearrange("l (r c) -> (l r) c", c=P)).then_inc(vec_landed.sem, 16)
            act.dma_start(vec_nat[NC_IN:NC_IN + KV, :], b_kv.rearrange("l (r c) -> (l r) c", c=P)).then_inc(vec_landed.sem, 16)
            for k, v in enumerate((conv_b, conv_ln_g, conv_ln_b, gmlp_ln_g, gmlp_ln_b)):
                at = NC_IN + KV + k * NG
                act.dma_start(vec_nat[at:at + NG, :], v.rearrange("l (r c) -> (l r) c", c=P)).then_inc(vec_landed.sem, 16)
            act.dma_start(cw_nat, conv_w.rearrange("l k c -> (l k) c")).then_inc(vec_landed.sem, 16)
            act.dma_start(ws_nat, gmlp_ws.rearrange("l h t s -> t (l h) s")).then_inc(ws_landed.sem, 16)
            act.dma_start(bs_bc, gmlp_bs.rearrange("l h t -> (l h t)").partition_broadcast(P)).then_inc(rows_landed.sem, 16)
            for dst, v in ((bout_bc, b_out), (lng_bc, ln_g), (lnb_bc, ln_b)):
                act.dma_start(dst[:], v.rearrange("l d -> (l d)").partition_broadcast(P)).then_inc(rows_landed.sem, 16)
            for i in range(MC):
                act.wait_ge(mem_turned.sem, i + 1)
                act.copy(x_hi[:, :, i * P:(i + 1) * P],
                         PS[:, 2 * i:2 * i + 2, :].rearrange("p a (k s) -> p (a k) s", s=P)).then_inc(mem_hi.sem, 1)
            for j in range(WR):
                weight_hi(0, j - KV)
            act.wait_ge(ws_turned.sem, 1)
            act.copy(wst[:, 0, :, :].rearrange("p (n h) s -> p n (h s)", n=2), PS[:, 6:8, 0:C2]).then_inc(ws_hi.sem, 1)
            act.wait_ge(vec_ready.sem, 2)
            for c in range(KV):
                act.wait_ge(*chunk_done(0, c - KV + 1))
                src = PS[:, 4 + c % 2, 0:MEM]
                dst = kt[:, 0, c, :] if c < NX else vt_nat[:, c - NX, :]
                act.activation(dst, src, ACT.Identity, bias=b_kv_col(c)).then_inc(kv_hi.sem, 1)
                weight_hi(0, c + WR - KV)
            act.wait_ge(v_back.sem, 1)
            act.copy(vm[:, 0, :, :], PS[:, 0:2, :]).then_inc(v_hi.sem, 1)

            def scalar_block(b, last):
                for j in range(NC_IN):
                    from_bank(b, j)
                    weight_hi(b, j + WR)
                    for kind, i in side.get(j, []):
                        side_stage(b, kind, i)
                    if j == NC_IN - 2:
                        y_hi(b, 0)
                        y_hi(b, 1)
                for e in range(NC_OUT):
                    if e + 2 < NC_OUT:
                        y_hi(b, e + 2)
                    if NC_IN + e + WR < CHUNKS or not last:
                        weight_hi(b, NC_IN + e + WR)
                if not last:
                    x_hi_tiles(b + 1)

            x_hi_tiles(0)
            with act.Fori(0, BLOCKS - 1) as b:
                scalar_block(b, False)
            scalar_block(BLOCKS - 1, True)

        @block.gpsimd
        def _(pool):
            def weight_lo(b, j):
                s = slot_of(j)
                pool.wait_ge(*w_hi(b, j + 1))
                pool.tensor_tensor(whl[:, s, 1, :], wstage[:, s, :], whl[:, s, 0, :].bitcast(F32),
                                   ALU.subtract).then_inc(w_split.sem, 1)

            def inv_std(b, n):
                pool.wait_ge(*ln_var(b, n + 1))
                pool.tensor_tensor(rstd[:, n:n + 1], ve[:, n:n + 1], neg_half[:], ALU.pow).then_inc(ln_rstd.sem, 1)

            def side_stage(b, kind, i):
                if kind == "v_turn":
                    inv_std(b, LN_V + i)
                    pool.wait_ge(*vn_hi(b, i + 1))
                    pool.tensor_tensor(v_norm(1, i), v_tmp, v_norm(0, i).bitcast(F32),
                                       ALU.subtract).then_inc(vn_split.sem, 1)
                elif kind == "c_turn":
                    inv_std(b, LN_C + i)

            def y_lo(b, e):
                pool.wait_ge(*y_hi_ready(b, e + 1))
                pool.tensor_tensor(y_part(1, e), y[:, y_order[e], :], y_part(0, e).bitcast(F32),
                                   ALU.subtract).then_inc(y_split.sem, 1)

            pool.memset(ident[:], 0.0).then_inc(idr.sem, 1)
            pool.memset(neg_half[:], -0.5)
            pool.wait_ge(idr.sem, 1)
            pool.affine_select(out=ident[:], in_=ident[:], compare_op=ALU.not_equal, fill=1.0, base=0,
                               pattern=[[-1, P]], channel_multiplier=1).then_inc(idr.sem, 1)
            pool.wait_ge(ws_landed.sem, 16)
            pool.affine_select(out=ws_low, in_=ws_nat, compare_op=ALU.is_ge, fill=0.0, base=0,
                               pattern=[[0, NH], [-1, P]], channel_multiplier=1).then_inc(msk.sem, 1)
            for j in range(-KV, WR):
                weight_lo(0, j)

            def gpsimd_block(b, last):
                for j in range(NC_IN):
                    weight_lo(b, j + WR)
                    for kind, i in side.get(j, []):
                        side_stage(b, kind, i)
                    if j == NC_IN - 2:
                        y_lo(b, 0)
                        y_lo(b, 1)
                for e in range(NC_OUT):
                    if e + 2 < NC_OUT:
                        y_lo(b, e + 2)
                    if NC_IN + e + WR < CHUNKS or not last:
                        weight_lo(b, NC_IN + e + WR)
                for t in range(T):
                    inv_std(b, LN_O + t)
                for t in range(T):
                    pool.wait_ge(*ln_done(b, t + 1))
                    pool.wait_ge(idr.sem, 2)
                    pool.dma_start(out_rows[bass.ds(b * B + t * P, P), :] if not last else
                                   out_rows[b * B + t * P:b * B + (t + 1) * P, :],
                                   res[:, t, :]).then_inc(stored[t].sem, 16)

            with pool.Fori(0, BLOCKS - 1) as b:
                gpsimd_block(b, False)
            gpsimd_block(BLOCKS - 1, True)

        @block.vector
        def _(dve):
            def x_lo_tiles(b):
                for t in range(T):
                    dve.wait_ge(*x_hi_ready(b, t + 1))
                    dve.tensor_tensor(x_lo[:, :, t * P:(t + 1) * P],
                                      pair_of("x_turn", t).rearrange("p a (k s) -> p (a k) s", s=P),
                                      x_hi[:, :, t * P:(t + 1) * P].bitcast(F32),
                                      ALU.subtract).then_inc(x_split.sem, 1)

            def from_bank(b, j):
                kind, i = order[j]
                src, bias = bank_of(j), b_in_col(first[kind] + i)
                if kind == "a":
                    n, s = tmp_of[("glu", i)], i % 2
                    dve.wait_ge(*conv_summed(b, i - 1))
                    dve.wait_ge(*halo_out(b, i + 1 - NG))
                    if i > 0:
                        dve.wait_ge(*halo_out(b, i))
                    dve.tensor_copy(h[:, s, 0:PAD], halo[:, i, :]).then_inc(halo_in.sem, 1)
                    dve.wait_ge(*chunk_done(b, j + 1))
                    dve.wait_ge(*tmp_full(b, n + 1))
                    dve.scalar_tensor_tensor(h[:, s, PAD:PAD + B], src, bias, gated[:, n % 2, :],
                                             ALU.add, ALU.mult).then_inc(tmp_used.sem, 1)
                    dve.wait_ge(*tmp_used(b, n + 1))
                    dve.tensor_copy(halo[:, i, :], h[:, s, B:B + PAD]).then_inc(halo_out.sem, 1)
                elif kind == "u":
                    n = tmp_of[order[j]]
                    dve.wait_ge(*tmp_full(b, n + 1))
                    dve.wait_ge(*mix_gated(b, i + 1))
                    dve.tensor_tensor(y[:, NG + i, :], y[:, NG + i, :], gated[:, n % 2, :],
                                      ALU.mult).then_inc(tmp_used.sem, 1)
                elif kind == "q":
                    dve.wait_ge(*q_hi_ready(b, i + 1))
                    dve.scalar_tensor_tensor(q_part(1, i), src, bias, q_part(0, i).bitcast(F32),
                                             ALU.add, ALU.subtract).then_inc(q_split.sem, 1)

            def tap(b, g, k):
                if k == TAPS:
                    dve.wait_ge(*tap_done(b, TAPS * (g + 1)))
                    dve.tensor_tensor(y[:, g, :], acc[1], even_sum[:], ALU.add).then_inc(conv_summed.sem, 1)
                    return
                src, w = h[:, g % 2, k:k + B], cw[:, g, k:k + 1]
                if k == 0:
                    dve.wait_ge(*tmp_used(b, tmp_of[("glu", g)] + 1))
                    dve.wait_ge(*conv_summed(b, g))
                    if g == 0:
                        dve.wait_ge(*res_summed(b, 0))
                    dve.tensor_scalar(acc[0], src, w, vec_col(CONV_B, g), ALU.mult, ALU.add).then_inc(tap_done.sem, 1)
                elif k == 1:
                    dve.tensor_scalar(acc[1], src, w, None, ALU.mult).then_inc(tap_done.sem, 1)
                else:
                    dve.wait_ge(*tap_done(b, TAPS * g + k - 1))
                    dve.scalar_tensor_tensor(even_sum[:] if k == TAPS - 1 else acc[k % 2], src, w,
                                             acc[k % 2], ALU.mult, ALU.add).then_inc(tap_done.sem, 1)

            def statistics(b, n, parts):
                for k, part in enumerate(parts):
                    dve.bn_stats(bn[:, n, k, :], part).then_inc(ln_stats.sem, 1)

            def moments(b, n):
                dve.wait_ge(*ln_stats(b, 2 * n + 2))
                dve.memset(ve[:, n:n + 1], EPS)
                dve.bn_aggr(mv[:, n, :], bn[:, n, :, :]).then_inc(ln_mean.sem, 1)
                dve.wait_ge(*ln_mean(b, n + 1))
                dve.tensor_tensor(ve[:, n:n + 1], ve[:, n:n + 1], mv[:, n, 1:2], ALU.add).then_inc(ln_var.sem, 1)

            def side_stage(b, kind, i):
                src = pair_of(kind, i)
                if kind in ("v_turn", "c_turn"):
                    n = (LN_V if kind == "v_turn" else LN_C) + i
                    dve.wait_ge(*(v_turned if kind == "v_turn" else c_turned)(b, i + 1))
                    statistics(b, n, (src[:, 0, 0:C2], src[:, 1, 0:C2]))
                    moments(b, n)
                elif kind == "mix":
                    dve.wait_ge(*mixed(b, i + 1))
                    for k, hd in enumerate((2 * i, 2 * i + 1)):
                        dve.scalar_tensor_tensor(
                            src[:, k, :].rearrange("p (t s) -> p t s", t=T),
                            src[:, k, :].rearrange("p (t s) -> p t s", t=T), vec_col(GMLP_G, hd),
                            mix_bias[:, hd:hd + 1, :].to_broadcast([P, T, P]),
                            ALU.mult, ALU.add).then_inc(mix_scaled.sem, 1)
                        dve.wait_ge(*mix_scaled(b, hd + 1))
                        dve.wait_ge(*gate_ready(b, gate_of[("gmlp_gate", hd)] + 1))
                        dve.tensor_tensor(y[:, NG + hd, :], src[:, k, :], y[:, NG + hd, :],
                                          ALU.mult).then_inc(mix_gated.sem, 1)
                elif kind == "score":
                    dve.wait_ge(*scored(b, i + 1))
                    dve.tensor_reduce(mx[:, i, :], src.rearrange("p a (t m) -> p (a t) m", t=2), AX.X,
                                      ALU.max).then_inc(max_ready.sem, 1)
                    dve.wait_ge(*max_ready(b, i + 1))
                    dve.tensor_scalar(nmx[:, i, :], mx[:, i, :], -SCALE, None, ALU.mult).then_inc(nmax_ready.sem, 1)
                    dve.wait_ge(*exp_done(b, i + 1))
                    dve.reciprocal(inv[:, i, :], sums[:, i, :]).then_inc(inv_ready.sem, 1)
                    dve.wait_ge(*inv_ready(b, i + 1))
                    dve.tensor_tensor(probs(i), probs(i),
                                      inv[:, i, :].rearrange("p (t o) -> p t o", o=1).to_broadcast([P, T, MEM]),
                                      ALU.mult).then_inc(p_ready.sem, 1)
                elif kind == "p_turn":
                    dve.wait_ge(*p_hi_ready(b, i + 1))
                    dve.tensor_tensor(p_part(1, i), src, p_part(0, i).bitcast(F32),
                                      ALU.subtract).then_inc(p_split.sem, 1)
                elif kind == "attend":
                    dve.wait_ge(*pv_done(b, i + 1))
                    dve.wait_ge(*gate_ready(b, gate_of[("x_gate", i)] + 1))
                    dve.tensor_tensor(y[:, NG + NH + i, :], src[:, 0, :], y[:, NG + NH + i, :],
                                      ALU.mult).then_inc(attended.sem, 1)
                elif kind == "c_back":
                    for c in (2 * i, 2 * i + 1):
                        dve.wait_ge(*gate_ready(b, gate_of[("conv_gate", c)] + 1))
                        dve.wait_ge(*tmp_full(b, tmp_of[("silu", c)] + 1))
                        dve.tensor_tensor(y[:, c, :], y[:, c, :], gated[:, tmp_of[("silu", c)] % 2, :],
                                          ALU.mult).then_inc(tmp_used.sem, 1)

            def normalise(b, kind, i):
                src = pair_of(kind, i)[:, :, 0:C2]
                n = (LN_V if kind == "v_turn" else LN_C) + i
                dst = v_tmp if kind == "v_turn" else c_norm(i)
                done = v_normed if kind == "v_turn" else c_normed
                dve.wait_ge(*ln_rstd(b, n + 1))
                if kind == "v_turn" and i > 0:
                    dve.wait_ge(*vn_split(b, i))
                dve.tensor_scalar(dst.rearrange("p (n c) -> p n c", n=2), src, mv[:, n, 0:1],
                                  rstd[:, n:n + 1], ALU.subtract, ALU.mult).then_inc(done.sem, 1)

            dve.memset(halo[:], 0.0).then_inc(halo_out.sem, 1)
            dve.memset(ones.bitcast(F32), 1.0)
            dve.wait_ge(vec_turned.sem, 1)
            dve.tensor_copy(cw[:].rearrange("p g k -> p (g k)"), PS[:, 5, 0:NG * TAPS]).then_inc(vec_ready.sem, 1)
            dve.tensor_copy(cols[:], PS[:, 4, 0:NV]).then_inc(vec_ready.sem, 1)
            for i in range(MC):
                dve.wait_ge(mem_hi.sem, i + 1)
                dve.tensor_tensor(x_lo[:, :, i * P:(i + 1) * P],
                                  PS[:, 2 * i:2 * i + 2, :].rearrange("p a (k s) -> p (a k) s", s=P),
                                  x_hi[:, :, i * P:(i + 1) * P].bitcast(F32), ALU.subtract).then_inc(mem_split.sem, 1)
            dve.wait_ge(ws_hi.sem, 1)
            dve.tensor_tensor(wst[:, 1, :, :].rearrange("p (n h) s -> p n (h s)", n=2), PS[:, 6:8, 0:C2],
                              wst[:, 0, :, :].rearrange("p (n h) s -> p n (h s)", n=2).bitcast(F32),
                              ALU.subtract).then_inc(ws_split.sem, 1)
            dve.wait_ge(vec_ready.sem, 2)
            for c in range(NX):
                dve.wait_ge(kv_hi.sem, c + 1)
                dve.scalar_tensor_tensor(kt[:, 1, c, :], PS[:, 4 + c % 2, 0:MEM], b_kv_col(c),
                                         kt[:, 0, c, :].bitcast(F32), ALU.add, ALU.subtract).then_inc(k_split.sem, 1)
            dve.wait_ge(row_sum.sem, 1)
            dve.wait_ge(rows_landed.sem, 4 * 16)
            for hd in range(NH):
                dve.scalar_tensor_tensor(mix_bias[:, hd, :], PS[:, 6 + hd // 3, hd % 3 * P:(hd % 3 + 1) * P],
                                         vec_col(GMLP_BETA, hd), bs_bc[:, hd * P:(hd + 1) * P],
                                         ALU.mult, ALU.add).then_inc(bias_ready.sem, 1)
            dve.wait_ge(v_hi.sem, 1)
            dve.tensor_tensor(vm[:, 1, :, :], PS[:, 0:2, :], vm[:, 0, :, :].bitcast(F32),
                              ALU.subtract).then_inc(v_split.sem, 1)
            dve.wait_ge(v_split.sem, 1)
            dve.wait_ge(bias_ready.sem, NH)
            dve.wait_ge(halo_out.sem, 1)
            dve.sem_inc(halo_out.sem, NG - 1)
            dve.sem_inc(tmp_used.sem, 2)
            dve.sem_inc(conv_summed.sem, 2)
            dve.sem_inc(res_summed.sem, T)
            dve.sem_inc(credit.sem, 1)

            def vector_block(b, last):
                for j in range(NC_IN):
                    from_bank(b, j)
                    for g, k in tap_plan.get(j, []):
                        tap(b, g, k)
                    for kind, i in side.get(j, []):
                        side_stage(b, kind, i)
                    for kind, i in side.get(j, []):
                        if kind in ("v_turn", "c_turn"):
                            normalise(b, kind, i)
                for t in range(T):
                    dve.wait_ge(*res_landed[t](b, 1))
                    dve.scalar_tensor_tensor(res[:, t, :], res[:, t, :], ALPHA, bout_bc[:],
                                             ALU.mult, ALU.add).then_inc(res_scaled.sem, 1)
                for t in range(T):
                    if t < T - 1:
                        dve.wait_ge(*out_ready(b, t + 1))
                    else:
                        dve.wait_ge(*chunk_done(b, CHUNKS))
                    dve.wait_ge(*res_scaled(b, t + 1))
                    dve.tensor_tensor(res[:, t, :], PS[:, 2 * t:2 * t + 2, :].rearrange("p a s -> p (a s)"),
                                      res[:, t, :], ALU.add).then_inc(res_summed.sem, 1)
                if not last:
                    x_lo_tiles(b + 1)
                for t in range(T):
                    dve.wait_ge(*res_summed(b, t + 1))
                    statistics(b, LN_O + t, (res[:, t, 0:HALF], res[:, t, HALF:D]))
                    moments(b, LN_O + t)
                    dve.scalar_tensor_tensor(res[:, t, :], res[:, t, :], mv[:, LN_O + t, 0:1], lng_bc[:],
                                             ALU.subtract, ALU.mult).then_inc(ln_scaled.sem, 1)
                    dve.wait_ge(*ln_scaled(b, t + 1))
                    dve.wait_ge(*ln_rstd(b, LN_O + t + 1))
                    dve.scalar_tensor_tensor(res[:, t, :], res[:, t, :], rstd[:, LN_O + t:LN_O + t + 1],
                                             lnb_bc[:], ALU.mult, ALU.add).then_inc(ln_done.sem, 1)

            x_lo_tiles(0)
            with dve.Fori(0, BLOCKS - 1) as b:
                vector_block(b, False)
            vector_block(BLOCKS - 1, True)


_INS = ["x", "mem", "w_in", "b_in", "conv_w", "conv_b", "conv_ln_g", "conv_ln_b", "gmlp_ln_g",
        "gmlp_ln_b", "gmlp_ws", "gmlp_bs", "w_kv", "b_kv", "w_out", "b_out", "ln_g", "ln_b"]


def kernel(**inputs):
    import numpy as np
    import concourse.bacc as bacc
    from concourse.bass_utils import run_bass_kernel_spmd

    nc = bacc.Bacc("TRN2", target_bir_lowering=False, num_devices=1)
    arrays, args = {}, []
    for name in _INS:
        a = np.ascontiguousarray(inputs[name])
        arrays[f"in_{name}"] = a
        args.append(nc.dram_tensor(f"in_{name}", a.shape, mybir.dt.from_np(a.dtype), kind="ExternalInput").ap())
    shape = arrays["in_x"].shape
    out = nc.dram_tensor("out_y", shape, F32, kind="ExternalOutput").ap()
    layer(nc, *args, out)
    r = run_bass_kernel_spmd(nc, [arrays], core_ids=[0])
    return r.results[0]["out_y"]
```

```python
from contextlib import ExitStack

import concourse.bass as bass
from concourse import mybir

P = 128
F32 = mybir.dt.float32
F32R = mybir.dt.float32r
ACT = mybir.ActivationFunctionType
ALU = mybir.AluOpType
AX = mybir.AxisListType


class Signal:

    def __init__(self, sem, per, lead=0, unit=1):
        self.sem, self.per, self.lead, self.unit = sem, per, lead, unit

    def __call__(self, b, n):
        return self.sem, b * (self.per * self.unit) + (self.lead + n) * self.unit


def layer(nc, x, mem, w_in, b_in, conv_w, conv_b, conv_ln_g, conv_ln_b, gmlp_ln_g, gmlp_ln_b,
          gmlp_ws, gmlp_bs, w_kv, b_kv, w_out, b_out, ln_g, ln_b, out):
    _, S, D = x.shape
    MEM = mem.shape[1]
    E_IN = w_in.shape[2]
    TAPS = conv_w.shape[1]
    DC = conv_w.shape[2]
    E_OUT = w_out.shape[1]
    DX = w_kv.shape[2] // 2
    KD = D // P
    NG = DC // P
    NH = gmlp_ws.shape[1]
    NX = DX // P
    MC = MEM // P
    B = 512
    T = B // P
    BLOCKS = S // B
    HALF = 512
    NC_IN = E_IN // P
    NC_OUT = E_OUT // P
    CHUNKS = NC_IN + NC_OUT
    KV = 2 * NX
    WR = 3
    PAD = TAPS - 1
    ALPHA = 2.0 ** 0.25
    EPS = 1e-5
    SCALE = float(P) ** -0.5
    C2 = DC // 2
    assert NG == 6 and NH == 6 and NX == 4 and KD == 8 and T == 4 and MC == 2 and D == 2 * HALF
    assert CHUNKS % WR == 0 and BLOCKS * B == S and DX == HALF

    order = []
    others = ([("v", c) for c in range(6)] + [("gmlp_gate", c) for c in range(6)]
              + [("q", c) for c in range(4)] + [("x_gate", c) for c in range(2)])
    for g in range(NG):
        order += [("glu", g), ("a", g)] + others[3 * g:3 * g + 3]
    order += [("x_gate", 2), ("x_gate", 3)] + [("u", c) for c in range(4)]
    order += [("conv_gate", c) for c in range(6)] + [("u", 4), ("u", 5)]
    assert len(order) == NC_IN
    first = {"a": 0, "glu": 6, "conv_gate": 12, "u": 18, "v": 24, "gmlp_gate": 30, "q": 36,
             "x_gate": 40}
    step_of = {k: j for j, k in enumerate(order)}
    y_order = list(range(6, 16)) + list(range(6))
    side = {10: [("v_turn", 0)], 11: [("v_turn", 1)], 12: [("v_turn", 2)], 13: [("v_turn", 3)],
            16: [("mix", 0)], 18: [("mix", 1)], 20: [("mix", 2)],
            23: [("score", 0)], 24: [("score", 1)], 25: [("p_turn", 0)], 26: [("p_turn", 1)],
            27: [("score", 2)], 28: [("score", 3)], 29: [("attend", 0)],
            30: [("attend", 1), ("p_turn", 2)], 31: [("p_turn", 3)], 32: [("attend", 2)], 33: [("attend", 3)],
            34: [("c_turn", 0), ("c_turn", 1)], 35: [("c_turn", 2), ("c_turn", 3)],
            38: [("c_back", 0)], 40: [("c_back", 1)], 41: [("c_back", 2)]}
    PAIR_USES = [("x_turn", t) for t in range(T)]
    for j in range(NC_IN):
        PAIR_USES += side.get(j, [])
    PAIR_USES += [("out", 0), ("out", 1)]
    assert len(PAIR_USES) % 2 == 0
    y_at = {38: 0, 39: 1, 40: 2, 41: 3}
    YR = 4
    OPEN = 5
    use_of = {k: u for u, k in enumerate(PAIR_USES)}
    tmp_uses = []
    for j in range(NC_IN):
        if order[j][0] in ("glu", "u"):
            tmp_uses.append(order[j])
        for kind, i in side.get(j, []):
            if kind == "c_back":
                tmp_uses += [("silu", 2 * i), ("silu", 2 * i + 1)]
    tmp_of = {k: i for i, k in enumerate(tmp_uses)}
    gate_of = {k: i for i, k in enumerate([o for o in order if "gate" in o[0]])}
    N_TMP = len(tmp_uses)
    LN_V, LN_C, LN_O = 0, T, 2 * T
    N_LN = 3 * T
    TAP_OPS = TAPS + 1
    tap_plan = {}
    for g in range(NG):
        n = 0
        for s, k in enumerate([7, 7, 6, 6, 6]):
            tap_plan[5 * g + 2 + s] = [(g, n + i) for i in range(k)]
            n += k
        assert n == TAP_OPS

    ctx = ExitStack()
    with ctx:
        def sb(name, shape, dt=F32):
            return ctx.enter_context(nc.sbuf_tensor(name, shape, dt))

        def signal(name, per=0, lead=0, unit=1):
            return Signal(ctx.enter_context(nc.semaphore(name)), per, lead, unit)

        PS = ctx.enter_context(nc.psum_tensor("banks", [P, 8, HALF], F32))
        x_hi = sb("x_hi", [P, KD, B], F32R)
        x_lo = sb("x_lo", [P, KD, B], F32R)
        whl = sb("w_split", [P, WR, 2, KD * P], F32R)
        kt = sb("k_split", [P, 2, NX, MEM], F32R)
        vm = sb("v_split", [P, 2, MC, DX], F32R)
        wst = sb("ws_split", [P, 2, NH, P], F32R)
        side_r = sb("side_split", [P, 2 * T * DC], F32R)
        wstage = sb("w_stage", [P, WR, KD * P])
        work = sb("work", [P, T * D])
        res = sb("residual", [P, T, D])
        y = sb("y_t", [P, NC_OUT, B])
        gated = sb("gated", [P, 2, B])
        h = sb("conv_in", [P, 2, PAD + B])
        halo = sb("halo", [P, NG, PAD])
        even_sum = sb("even_sum", [P, B])
        ident = sb("ident", [P, P])
        mix_bias = sb("mix_bias", [P, NH, P])
        bout_bc = sb("b_out_rows", [P, D])
        lng_bc = sb("ln_g_rows", [P, D])
        lnb_bc = sb("ln_b_rows", [P, D])
        NV = NC_IN + KV + 5 * NG
        cols = sb("vector_columns", [P, NV])
        cw = sb("conv_w_columns", [P, NG, TAPS])
        neg_half = sb("neg_half", [P, 1])
        bn = sb("bn", [P, N_LN, 2, 6])
        mv = sb("mean_var", [P, N_LN, 2])
        ve = sb("var_eps", [P, N_LN])
        rstd = sb("rstd", [P, N_LN])
        mx = sb("score_max", [P, NX, T])
        nmx = sb("neg_max", [P, NX, T])
        sums = sb("exp_sums", [P, NX, T])
        inv = sb("inv_sums", [P, NX, T])

        yf = y[:].rearrange("p c s -> p (c s)")
        cw_nat = yf[0:TAPS, 0:DC]
        ws_nat = yf[:, DC:2 * DC].rearrange("p (h s) -> p h s", h=NH)
        ws_low = yf[:, 2 * DC:3 * DC].rearrange("p (h s) -> p h s", h=NH)
        bs_bc = yf[:, 3 * DC:4 * DC]
        vec_nat = yf[0:NV, 4 * DC:4 * DC + P]
        vt_nat = yf[:, 8 * HALF:8 * HALF + NX * MEM].rearrange("p (h m) -> p h m", h=NX)
        ones = side_r[:, 0:P]

        b_in_col = lambda c: cols[:, c:c + 1]
        b_kv_col = lambda c: cols[:, NC_IN + c:NC_IN + c + 1]
        vec_col = lambda k, c: cols[:, NC_IN + KV + k * NG + c:NC_IN + KV + k * NG + c + 1]
        CONV_B, CONV_G, CONV_BETA, GMLP_G, GMLP_BETA = range(5)

        def v_norm(part, t):
            return side_r[:, (part * T + t) * DC:(part * T + t + 1) * DC]

        def q_part(part, hd):
            return side_r[:, (hd % 2 * 2 + part) * B:(hd % 2 * 2 + part + 1) * B]

        def p_part(part, hd):
            at = 4 * B + (hd % 2 * 2 + part) * MC * B
            return side_r[:, at:at + MC * B].rearrange("p (c s) -> p c s", c=MC)

        def y_part(part, e):
            at = 4 * B + (e % YR * 2 + part) * B
            return side_r[:, at:at + B]

        x_tile = lambda t: work[:, t * D:(t + 1) * D]
        v_act = lambda c: work[:, c * B:(c + 1) * B]
        v_tmp = work[:, NH * B:NH * B + DC]
        probs = lambda hd: work[:, hd % 2 * T * MEM:(hd % 2 + 1) * T * MEM].rearrange(
            "p (t m) -> p t m", t=T)
        c_norm = lambda t: work[:, t * DC:(t + 1) * DC]

        def pair_of(kind, i):
            p = use_of[(kind, i)] % 2
            return PS[:, 2 * p:2 * p + 2, :]

        def bank_of(j):
            return PS[:, 4 + j % 2, :]

        acc = [PS[:, 6, :], PS[:, 7, :]]

        mem_landed = signal("mem_landed")
        vec_landed = signal("vectors_landed")
        ws_landed = signal("ws_landed")
        rows_landed = signal("rows_landed")
        idr = signal("identity_ready")
        msk = signal("ws_masked")
        credit = signal("credits_given")
        vec_turned = signal("vectors_turned")
        vec_ready = signal("vectors_ready")
        mem_turned = signal("mem_turned")
        mem_hi = signal("mem_hi_ready")
        mem_split = signal("mem_split_ready")
        ws_turned = signal("ws_turned")
        ws_hi = signal("ws_hi_ready")
        ws_split = signal("ws_split_ready")
        row_sum = signal("ws_row_sums")
        bias_ready = signal("mix_bias_ready")
        kv_hi = signal("k_hi_or_v_ready")
        k_split = signal("k_split_ready")
        v_back = signal("v_memory_turned")
        v_hi = signal("v_memory_hi")
        v_split = signal("v_memory_split")

        w_landed = [signal(f"w_landed{s}", CHUNKS // WR, 0, 16) for s in range(WR)]
        w_hi = signal("w_hi_ready", CHUNKS, KV)
        w_split = signal("w_split_ready", CHUNKS, KV)
        chunk_done = signal("chunk_done", CHUNKS, KV)
        x_landed = [signal(f"x_landed{t}", 1, 0, 16) for t in range(T)]
        res_landed = [signal(f"residual_landed{t}", 1, 0, 16) for t in range(T)]
        stored = [signal(f"out_stored{t}", 1, 0, 16) for t in range(T)]
        x_turned = signal("x_turned", T)
        x_hi_ready = signal("x_hi_ready", T)
        x_split = signal("x_split_ready", T)
        tmp_full = signal("gated_full", N_TMP)
        tmp_used = signal("gated_used", N_TMP, 2)
        v_ready = signal("v_ready", NH)
        gate_ready = signal("gate_ready", len(gate_of))
        q_hi_ready = signal("q_hi_ready", NX)
        q_split = signal("q_split_ready", NX)
        halo_in = signal("halo_in", NG)
        halo_out = signal("halo_out", NG, NG)
        tap_done = signal("tap_done", NG * TAPS)
        conv_summed = signal("conv_summed", NG, 2)
        v_turned = signal("v_turned", T)
        v_normed = signal("v_normed", T)
        vn_hi = signal("v_norm_hi", T)
        vn_split = signal("v_norm_split", T)
        ln_stats = signal("ln_stats", 2 * N_LN)
        ln_mean = signal("ln_mean", N_LN)
        ln_var = signal("ln_var_eps", N_LN)
        ln_rstd = signal("ln_rstd", N_LN)
        mixed = signal("mixed", NH // 2)
        mix_scaled = signal("mix_scaled", NH)
        mix_gated = signal("mix_gated", NH)
        scored = signal("scored", NX)
        max_ready = signal("max_ready", NX)
        nmax_ready = signal("neg_max_ready", NX)
        exp_done = signal("exp_done", NX)
        inv_ready = signal("inv_ready", NX)
        p_ready = signal("probs_ready", NX)
        p_turned = signal("probs_turned", NX)
        p_hi_ready = signal("probs_hi_ready", NX)
        p_split = signal("probs_split_ready", NX)
        pv_done = signal("pv_done", NX)
        attended = signal("attended", NX)
        c_turned = signal("conv_turned", T)
        c_normed = signal("conv_normed", T)
        c_back = signal("conv_back", NG // 2)
        y_hi_ready = signal("y_hi_ready", NC_OUT)
        y_split = signal("y_split_ready", NC_OUT)
        out_ready = signal("out_ready", T - 1)
        res_scaled = signal("residual_scaled", T)
        res_summed = signal("residual_summed", T, T)
        ln_scaled = signal("out_ln_scaled", T)
        ln_done = signal("out_ln_done", T)

        def bank_released(b, j):
            kind, i = order[j]
            if kind in ("glu", "u"):
                return tmp_full(b, tmp_of[order[j]] + 1)
            if kind == "a":
                return tmp_used(b, tmp_of[("glu", i)] + 1)
            if kind == "v":
                return v_ready(b, i + 1)
            if kind == "q":
                return q_split(b, i + 1)
            return gate_ready(b, gate_of[order[j]] + 1)

        def pair_released(b, u):
            kind, i = PAIR_USES[u]
            return {
                "x_turn": lambda: x_split(b, i + 1),
                "v_turn": lambda: v_normed(b, i + 1),
                "mix": lambda: mix_gated(b, 2 * i + 2),
                "score": lambda: exp_done(b, i + 1),
                "p_turn": lambda: p_split(b, i + 1),
                "attend": lambda: attended(b, i + 1),
                "c_turn": lambda: c_normed(b, i + 1),
                "c_back": lambda: tmp_full(b, tmp_of[("silu", 2 * i + 1)] + 1),
                "out": lambda: res_summed(b, i + 1 - T),
            }[kind]()

        def y_final(b, c):
            if c < NG:
                return tmp_used(b, tmp_of[("silu", c)] + 1)
            if c < NG + NH:
                return tmp_used(b, tmp_of[("u", c - NG)] + 1)
            return attended(b, c - NG - NH + 1)

        slot_of = lambda j: (KV + j) % WR

        x_rows = x.rearrange("o s d -> (o s) d")
        out_rows = out.rearrange("o s d -> (o s) d")
        w_in_v = w_in.rearrange("l (k p) e -> p (l k) e", p=P)
        w_kv_v = w_kv.rearrange("l (k p) e -> p (l k) e", p=P)
        w_out_v = w_out.rearrange("l e n -> (l e) n")
        mem_rows = mem.rearrange("o m d -> (o m) d")

        block = ctx.enter_context(nc.Block())

        @block.sync
        def _(sp):
            def load_w(b, j):
                s = slot_of(j)
                if not (isinstance(b, int) and b == 0 and KV + j < WR):
                    sp.wait_ge(*w_split(b, j - WR + 1))
                dst = wstage[:, s, :]
                if j < 0:
                    src = w_kv_v[:, :, (KV + j) * P:(KV + j + 1) * P]
                elif j < NC_IN:
                    kind, i = order[j]
                    c = first[kind] + i
                    src = w_in_v[:, :, c * P:(c + 1) * P]
                else:
                    c = y_order[j - NC_IN]
                    sp.dma_start(dst, w_out_v[c * P:(c + 1) * P, :]).then_inc(w_landed[s].sem, 16)
                    return
                sp.dma_start(dst.rearrange("p (k e) -> p k e", k=KD), src).then_inc(w_landed[s].sem, 16)

            def load_x(b, t):
                sp.dma_start(x_tile(t), x_rows[bass.ds(b * B + t * P, P), :]).then_inc(x_landed[t].sem, 16)

            def load_rows(b, t, behind):
                if behind:
                    sp.wait_ge(*stored[t](b, 0))
                sp.dma_start(res[:, t, :], x_rows[bass.ds(b * B + t * P, P), :]).then_inc(
                    res_landed[t].sem, 16)

            for i in range(MC):
                sp.dma_start(res[:, i, :], mem_rows[i * P:(i + 1) * P, :]).then_inc(mem_landed.sem, 16)
            load_w(0, -KV)
            load_w(0, 1 - KV)
            load_w(0, 2 - KV)
            for t in range(T):
                sp.dma_start(x_tile(t), x_rows[t * P:(t + 1) * P, :]).then_inc(x_landed[t].sem, 16)
            for j in range(WR - KV, 0):
                load_w(0, j)

            rows_at, x_at = (24, 27, 30, 33), (47, 49, 51, 53)

            def sync_block(b, last):
                for j in range(CHUNKS):
                    load_w(b, j)
                    if j in rows_at and last:
                        load_rows(b, rows_at.index(j), True)
                    elif j in rows_at:
                        with sp.If(b > 0):
                            load_rows(b, rows_at.index(j), True)
                        with sp.Else():
                            load_rows(b, rows_at.index(j), False)
                    if j in x_at and not last:
                        if j == x_at[0]:
                            sp.wait_ge(*c_back(b, NG // 2))
                        load_x(b + 1, x_at.index(j))

            sp.wait_ge(mem_turned.sem, MC)
            with sp.Fori(0, BLOCKS - 1) as b:
                sync_block(b, False)
            sync_block(BLOCKS - 1, True)
            for t in range(T):
                sp.wait_ge(*stored[t](BLOCKS - 1, 1))

        @block.tensor
        def _(pe):
            def turn_x(b, t):
                pe.wait_ge(*x_landed[t](b, 1))
                pe.wait_ge(*(pair_released(b, use_of[("x_turn", t)] - 2)))
                dst = pair_of("x_turn", t)
                for k in range(KD):
                    m = pe.transpose(dst[:, k // 4, k % 4 * P:(k % 4 + 1) * P],
                                     x_tile(t)[:, k * P:(k + 1) * P], ident[:])
                m.then_inc(x_turned.sem, 1)

            def product(dst, w, moving_hi, moving_lo, steps, n_inc):
                for k in range(steps):
                    pe.matmul(dst, w(0, k), moving_hi(k), start=(k == 0), stop=False)
                    pe.matmul(dst, w(0, k), moving_lo(k), start=False, stop=False)
                    m = pe.matmul(dst, w(1, k), moving_hi(k), start=False, stop=(k == steps - 1))
                if n_inc is not None:
                    m.then_inc(n_inc.sem, 1)

            def project(b, j):
                s = slot_of(j)
                pe.wait_ge(*w_split(b, j + 1))
                if j < 2:
                    pe.wait_ge(*res_summed(b, 3 - T))
                else:
                    pe.wait_ge(*bank_released(b, j - 2))
                if j == 0:
                    for n in range(2):
                        pe.wait_ge(*x_split(b, 2 * n + 2))
                        at = slice(n * 2 * P, (n + 1) * 2 * P)
                        product(bank_of(j)[:, at], lambda part, k: whl[:, s, part, k * P:(k + 1) * P],
                                lambda k: x_hi[:, k, at], lambda k: x_lo[:, k, at], KD,
                                chunk_done if n == 1 else None)
                    return
                product(bank_of(j), lambda part, k: whl[:, s, part, k * P:(k + 1) * P],
                        lambda k: x_hi[:, k, :], lambda k: x_lo[:, k, :], KD, chunk_done)

            def side_stage(b, kind, i):
                pe.wait_ge(*pair_released(b, use_of[(kind, i)] - 2))
                dst = pair_of(kind, i)
                if kind == "v_turn":
                    pe.wait_ge(*v_ready(b, NH))
                    for c in range(NH):
                        m = pe.transpose(dst[:, c // 3, c % 3 * P:(c % 3 + 1) * P],
                                         v_act(c)[:, i * P:(i + 1) * P], ident[:])
                    m.then_inc(v_turned.sem, 1)
                elif kind == "mix":
                    pe.wait_ge(*vn_split(b, T))
                    for n, hd in enumerate((2 * i, 2 * i + 1)):
                        for t in range(T):
                            d = dst[:, n, t * P:(t + 1) * P]
                            vh = v_norm(0, t)[:, hd * P:(hd + 1) * P]
                            vl = v_norm(1, t)[:, hd * P:(hd + 1) * P]
                            pe.matmul(d, vh, wst[:, 0, hd, :], start=True, stop=False)
                            pe.matmul(d, vh, wst[:, 1, hd, :], start=False, stop=False)
                            m = pe.matmul(d, vl, wst[:, 0, hd, :], start=False, stop=True)
                    m.then_inc(mixed.sem, 1)
                elif kind == "score":
                    pe.wait_ge(*q_split(b, i + 1))
                    for t in range(T):
                        d = dst[:, t // 2, t % 2 * MEM:(t % 2 + 1) * MEM]
                        qh = q_part(0, i)[:, t * P:(t + 1) * P]
                        ql = q_part(1, i)[:, t * P:(t + 1) * P]
                        pe.matmul(d, qh, kt[:, 0, i, :], start=True, stop=False)
                        pe.matmul(d, qh, kt[:, 1, i, :], start=False, stop=False)
                        m = pe.matmul(d, ql, kt[:, 0, i, :], start=False, stop=True)
                    m.then_inc(scored.sem, 1)
                elif kind == "p_turn":
                    pe.wait_ge(*p_ready(b, i + 1))
                    for c in range(MC):
                        for t in range(T):
                            m = pe.transpose(dst[:, c, t * P:(t + 1) * P],
                                             probs(i)[:, t, c * P:(c + 1) * P], ident[:])
                    m.then_inc(p_turned.sem, 1)
                elif kind == "attend":
                    pe.wait_ge(*p_split(b, i + 1))
                    product(dst[:, 0, :], lambda part, k: vm[:, part, k, i * P:(i + 1) * P],
                            lambda k: p_part(0, i)[:, k, :], lambda k: p_part(1, i)[:, k, :],
                            MC, pv_done)
                elif kind == "c_turn":
                    pe.wait_ge(*conv_summed(b, NG))
                    for c in range(NG):
                        m = pe.transpose(dst[:, c // 3, c % 3 * P:(c % 3 + 1) * P],
                                         y[:, c, i * P:(i + 1) * P], ident[:])
                    m.then_inc(c_turned.sem, 1)
                elif kind == "c_back":
                    pe.wait_ge(*c_normed(b, T))
                    for n, c in enumerate((2 * i, 2 * i + 1)):
                        for t in range(T):
                            m = pe.transpose(dst[:, n, t * P:(t + 1) * P],
                                             c_norm(t)[:, c * P:(c + 1) * P], ident[:])
                    m.then_inc(c_back.sem, 1)

            def project_out(b, e, t):
                s = slot_of(NC_IN + e)
                yh = y_part(0, e)[:, t * P:(t + 1) * P]
                yl = y_part(1, e)[:, t * P:(t + 1) * P]
                for n in range(2):
                    d = PS[:, 2 * t + n, :]
                    wh = whl[:, s, 0, n * HALF:(n + 1) * HALF]
                    wl = whl[:, s, 1, n * HALF:(n + 1) * HALF]
                    pe.matmul(d, yh, wh, start=(e == 0), stop=False)
                    pe.matmul(d, yh, wl, start=False, stop=False)
                    m = pe.matmul(d, yl, wh, start=False, stop=(e == NC_OUT - 1))
                return m

            pe.wait_ge(idr.sem, 2)
            pe.wait_ge(vec_landed.sem, 8 * 16)
            pe.transpose(PS[:, 4, 0:NV], vec_nat, ident[0:NV, 0:NV])
            for g in range(NG):
                m = pe.transpose(PS[:, 5, g * TAPS:(g + 1) * TAPS], cw_nat[:, g * P:(g + 1) * P],
                                 ident[0:TAPS, 0:TAPS])
            m.then_inc(vec_turned.sem, 1)
            pe.wait_ge(mem_landed.sem, MC * 16)
            for i in range(MC):
                for k in range(KD):
                    m = pe.transpose(PS[:, 2 * i + k // 4, k % 4 * P:(k % 4 + 1) * P],
                                     res[:, i, k * P:(k + 1) * P], ident[:])
                m.then_inc(mem_turned.sem, 1)
            pe.wait_ge(msk.sem, 1)
            for hd in range(NH):
                m = pe.transpose(PS[:, 6 + hd // 3, hd % 3 * P:(hd % 3 + 1) * P], ws_low[:, hd, :],
                                 ident[:])
            m.then_inc(ws_turned.sem, 1)
            pe.wait_ge(mem_split.sem, MC)
            pe.wait_ge(vec_ready.sem, 2)
            for c in range(KV):
                pe.wait_ge(*w_split(0, c - KV + 1))
                if c >= 2:
                    if c - 2 < NX:
                        pe.wait_ge(k_split.sem, c - 1)
                    else:
                        pe.wait_ge(kv_hi.sem, c - 1)
                s = c % WR
                product(PS[:, 4 + c % 2, 0:MEM], lambda part, k: whl[:, s, part, k * P:(k + 1) * P],
                        lambda k: x_hi[:, k, 0:MEM], lambda k: x_lo[:, k, 0:MEM], KD, chunk_done)
            pe.wait_ge(ws_split.sem, 1)
            for n in range(2):
                for part in range(2):
                    m = pe.matmul(PS[:, 6 + n, 0:C2], ones,
                                  wst[:, part, 3 * n:3 * n + 3, :], start=(part == 0), stop=(part == 1))
            m.then_inc(row_sum.sem, 1)
            pe.wait_ge(kv_hi.sem, KV)
            for c in range(MC):
                for hd in range(NX):
                    m = pe.transpose(PS[:, c, hd * P:(hd + 1) * P], vt_nat[:, hd, c * P:(c + 1) * P],
                                     ident[:])
            m.then_inc(v_back.sem, 1)
            pe.wait_ge(v_split.sem, 1)
            pe.wait_ge(bias_ready.sem, NH)
            pe.wait_ge(credit.sem, 1)

            def tensor_block(b, last):
                for j in range(NC_IN):
                    project(b, j)
                    for kind, i in side.get(j, []):
                        side_stage(b, kind, i)
                for e in range(NC_OUT - 2):
                    pe.wait_ge(*w_split(b, NC_IN + e + 1))
                    pe.wait_ge(*y_split(b, e + 1))
                    for t in range(T):
                        if e == 0 and t < 2:
                            pe.wait_ge(*pair_released(b, use_of[("out", t)] - 2))
                        elif e == 0 and t == 2:
                            pe.wait_ge(*bank_released(b, NC_IN - 2))
                            pe.wait_ge(*bank_released(b, NC_IN - 1))
                        elif e == 0:
                            pe.wait_ge(*conv_summed(b, NG))
                        m = project_out(b, e, t)
                    m.then_inc(chunk_done.sem, 1)
                pe.wait_ge(*w_split(b, CHUNKS))
                pe.wait_ge(*y_split(b, NC_OUT))
                for t in range(T - 1):
                    project_out(b, NC_OUT - 2, t)
                    m = project_out(b, NC_OUT - 1, t)
                    m.then_inc(out_ready.sem, 1)
                    if t > 0 and not last:
                        turn_x(b + 1, t - 1)
                m = project_out(b, NC_OUT - 2, T - 1)
                m.then_inc(chunk_done.sem, 1)
                if not last:
                    turn_x(b + 1, T - 2)
                m = project_out(b, NC_OUT - 1, T - 1)
                m.then_inc(chunk_done.sem, 1)
                if not last:
                    turn_x(b + 1, T - 1)

            for t in range(T):
                turn_x(0, t)
            with pe.Fori(0, BLOCKS - 1) as b:
                tensor_block(b, False)
            tensor_block(BLOCKS - 1, True)

        @block.scalar
        def _(act):
            def weight_hi(b, j):
                s = slot_of(j)
                n = (KV + j) // WR + 1
                act.wait_ge(w_landed[s].sem, b * (16 * (CHUNKS // WR)) + 16 * n)
                if not (isinstance(b, int) and b == 0 and KV + j < WR):
                    act.wait_ge(*chunk_done(b, j - WR + 1))
                act.copy(whl[:, s, 0, :], wstage[:, s, :]).then_inc(w_hi.sem, 1)

            def x_hi_tile(b, t):
                act.wait_ge(*x_turned(b, t + 1))
                act.copy(x_hi[:, :, t * P:(t + 1) * P],
                         pair_of("x_turn", t).rearrange("p a (k s) -> p (a k) s", s=P)).then_inc(
                    x_hi_ready.sem, 1)

            def from_bank(b, j):
                kind, i = order[j]
                src, bias = bank_of(j), b_in_col(first[kind] + i)
                if kind == "a":
                    return
                act.wait_ge(*chunk_done(b, j + 1))
                if kind in ("glu", "u"):
                    n = tmp_of[order[j]]
                    act.wait_ge(*tmp_used(b, n - 1))
                    act.activation(gated[:, n % 2, :], src,
                                   ACT.Sigmoid if kind == "glu" else ACT.Gelu_apprx_tanh,
                                   bias=bias).then_inc(tmp_full.sem, 1)
                elif kind == "v":
                    act.activation(v_act(i), src, ACT.Gelu_apprx_tanh, bias=bias).then_inc(v_ready.sem, 1)
                elif kind == "q":
                    act.activation(q_part(0, i), src, ACT.Identity, bias=bias).then_inc(q_hi_ready.sem, 1)
                else:
                    c = {"conv_gate": 0, "gmlp_gate": NG, "x_gate": NG + NH}[kind] + i
                    act.activation(y[:, c, :], src, ACT.Silu, bias=bias).then_inc(gate_ready.sem, 1)

            def v_norm_hi(b, i):
                act.wait_ge(*v_normed(b, i + 1))
                act.copy(v_norm(0, i), v_tmp).then_inc(vn_hi.sem, 1)

            def side_stage(b, kind, i):
                if kind == "score":
                    act.wait_ge(*scored(b, i + 1))
                    act.wait_ge(*nmax_ready(b, i + 1))
                    for t in range(T):
                        m = act.activation(probs(i)[:, t, :],
                                           pair_of(kind, i)[:, t // 2, t % 2 * MEM:(t % 2 + 1) * MEM],
                                           ACT.Exp, bias=nmx[:, i, t:t + 1], scale=SCALE,
                                           accum_out=sums[:, i, t:t + 1])
                    m.then_inc(exp_done.sem, 1)
                elif kind == "p_turn":
                    act.wait_ge(*p_turned(b, i + 1))
                    act.copy(p_part(0, i), pair_of(kind, i)).then_inc(p_hi_ready.sem, 1)
                elif kind == "c_back":
                    act.wait_ge(*c_back(b, i + 1))
                    for n, c in enumerate((2 * i, 2 * i + 1)):
                        k = tmp_of[("silu", c)]
                        act.wait_ge(*tmp_used(b, k - 1))
                        act.activation(gated[:, k % 2, :], pair_of(kind, i)[:, n, :], ACT.Silu,
                                       bias=vec_col(CONV_BETA, c), scale=vec_col(CONV_G, c)).then_inc(
                            tmp_full.sem, 1)

            def y_hi(b, e):
                if e >= YR:
                    act.wait_ge(*chunk_done(b, NC_IN + e - YR + 1))
                act.wait_ge(*y_final(b, y_order[e]))
                act.copy(y_part(0, e), y[:, y_order[e], :]).then_inc(y_hi_ready.sem, 1)

            act.dma_start(vec_nat[0:NC_IN, :], b_in.rearrange("l (r c) -> (l r) c", c=P)).then_inc(vec_landed.sem, 16)
            act.dma_start(vec_nat[NC_IN:NC_IN + KV, :], b_kv.rearrange("l (r c) -> (l r) c", c=P)).then_inc(vec_landed.sem, 16)
            for k, v in enumerate((conv_b, conv_ln_g, conv_ln_b, gmlp_ln_g, gmlp_ln_b)):
                at = NC_IN + KV + k * NG
                act.dma_start(vec_nat[at:at + NG, :], v.rearrange("l (r c) -> (l r) c", c=P)).then_inc(vec_landed.sem, 16)
            act.dma_start(cw_nat, conv_w.rearrange("l k c -> (l k) c")).then_inc(vec_landed.sem, 16)
            act.dma_start(ws_nat, gmlp_ws.rearrange("l h t s -> t (l h) s")).then_inc(ws_landed.sem, 16)
            act.dma_start(bs_bc, gmlp_bs.rearrange("l h t -> (l h t)").partition_broadcast(P)).then_inc(rows_landed.sem, 16)
            for dst, v in ((bout_bc, b_out), (lng_bc, ln_g), (lnb_bc, ln_b)):
                act.dma_start(dst[:], v.rearrange("l d -> (l d)").partition_broadcast(P)).then_inc(rows_landed.sem, 16)
            for i in range(MC):
                act.wait_ge(mem_turned.sem, i + 1)
                act.copy(x_hi[:, :, i * P:(i + 1) * P],
                         PS[:, 2 * i:2 * i + 2, :].rearrange("p a (k s) -> p (a k) s", s=P)).then_inc(mem_hi.sem, 1)
            for j in range(WR):
                weight_hi(0, j - KV)
            act.wait_ge(ws_turned.sem, 1)
            act.copy(wst[:, 0, :, :].rearrange("p (n h) s -> p n (h s)", n=2), PS[:, 6:8, 0:C2]).then_inc(ws_hi.sem, 1)
            act.wait_ge(vec_ready.sem, 2)
            for c in range(KV):
                act.wait_ge(*chunk_done(0, c - KV + 1))
                src = PS[:, 4 + c % 2, 0:MEM]
                dst = kt[:, 0, c, :] if c < NX else vt_nat[:, c - NX, :]
                act.activation(dst, src, ACT.Identity, bias=b_kv_col(c)).then_inc(kv_hi.sem, 1)
                weight_hi(0, c + WR - KV)
            act.wait_ge(v_back.sem, 1)
            act.copy(vm[:, 0, :, :], PS[:, 0:2, :]).then_inc(v_hi.sem, 1)

            def scalar_block(b, last):
                for j in range(NC_IN):
                    from_bank(b, j)
                    weight_hi(b, j + WR)
                    for kind, i in side.get(j - 1, []):
                        if kind == "v_turn":
                            v_norm_hi(b, i)
                    for kind, i in side.get(j, []):
                        side_stage(b, kind, i)
                    if j in y_at:
                        y_hi(b, y_at[j])
                for e in range(NC_OUT):
                    if NC_IN + e + WR < CHUNKS:
                        weight_hi(b, NC_IN + e + WR)
                    if e + YR < NC_OUT:
                        y_hi(b, e + YR)
                if not last:
                    weight_hi(b, CHUNKS)
                    x_hi_tile(b + 1, 0)
                    x_hi_tile(b + 1, 1)
                    x_hi_tile(b + 1, 2)
                    weight_hi(b, CHUNKS + 1)
                    x_hi_tile(b + 1, 3)
                    weight_hi(b, CHUNKS + 2)

            for t in range(T):
                x_hi_tile(0, t)
            with act.Fori(0, BLOCKS - 1) as b:
                scalar_block(b, False)
            scalar_block(BLOCKS - 1, True)

        @block.gpsimd
        def _(pool):
            def weight_lo(b, j):
                s = slot_of(j)
                pool.wait_ge(*w_hi(b, j + 1))
                pool.tensor_tensor(whl[:, s, 1, :], wstage[:, s, :], whl[:, s, 0, :].bitcast(F32),
                                   ALU.subtract).then_inc(w_split.sem, 1)

            def inv_std(b, n):
                pool.wait_ge(*ln_var(b, n + 1))
                pool.tensor_tensor(rstd[:, n:n + 1], ve[:, n:n + 1], neg_half[:], ALU.pow).then_inc(ln_rstd.sem, 1)

            def side_stage(b, kind, i):
                if kind == "v_turn":
                    inv_std(b, LN_V + i)
                elif kind == "c_turn":
                    inv_std(b, LN_C + i)

            def v_norm_lo(b, i):
                pool.wait_ge(*vn_hi(b, i + 1))
                pool.tensor_tensor(v_norm(1, i), v_tmp, v_norm(0, i).bitcast(F32),
                                   ALU.subtract).then_inc(vn_split.sem, 1)

            def store(b, t):
                pool.wait_ge(*ln_done(b, t + 1))
                pool.dma_start(out_rows[bass.ds(b * B + t * P, P), :],
                               res[:, t, :]).then_inc(stored[t].sem, 16)

            pool.memset(ident[:], 0.0).then_inc(idr.sem, 1)
            pool.memset(neg_half[:], -0.5)
            pool.wait_ge(idr.sem, 1)
            pool.affine_select(out=ident[:], in_=ident[:], compare_op=ALU.not_equal, fill=1.0, base=0,
                               pattern=[[-1, P]], channel_multiplier=1).then_inc(idr.sem, 1)
            pool.wait_ge(ws_landed.sem, 16)
            pool.affine_select(out=ws_low, in_=ws_nat, compare_op=ALU.is_ge, fill=0.0, base=0,
                               pattern=[[0, NH], [-1, P]], channel_multiplier=1).then_inc(msk.sem, 1)
            for j in range(-KV, WR):
                weight_lo(0, j)

            def step(b, j):
                weight_lo(b, j + WR)
                for kind, i in side.get(j - 1, []):
                    if kind == "v_turn":
                        v_norm_lo(b, i)
                for kind, i in side.get(j, []):
                    side_stage(b, kind, i)

            def gpsimd_block(b, last):
                for j in range(OPEN, NC_IN):
                    step(b, j)
                for j in range(NC_IN, CHUNKS if not last else CHUNKS - WR):
                    weight_lo(b, j + WR)
                inv_std(b, LN_O)
                inv_std(b, LN_O + 1)
                if not last:
                    step(b + 1, 0)
                store(b, 0)
                store(b, 1)
                if not last:
                    step(b + 1, 1)
                    step(b + 1, 2)
                inv_std(b, LN_O + 2)
                if not last:
                    step(b + 1, 3)
                inv_std(b, LN_O + 3)
                store(b, 2)
                if not last:
                    step(b + 1, 4)
                store(b, 3)

            for j in range(OPEN):
                step(0, j)
            with pool.Fori(0, BLOCKS - 1) as b:
                gpsimd_block(b, False)
            gpsimd_block(BLOCKS - 1, True)

        @block.vector
        def _(dve):
            def x_lo_tile(b, t):
                dve.wait_ge(*x_hi_ready(b, t + 1))
                dve.tensor_tensor(x_lo[:, :, t * P:(t + 1) * P],
                                  pair_of("x_turn", t).rearrange("p a (k s) -> p (a k) s", s=P),
                                  x_hi[:, :, t * P:(t + 1) * P].bitcast(F32),
                                  ALU.subtract).then_inc(x_split.sem, 1)

            def from_bank(b, j):
                kind, i = order[j]
                src, bias = bank_of(j), b_in_col(first[kind] + i)
                if kind == "a":
                    n, s = tmp_of[("glu", i)], i % 2
                    dve.wait_ge(*conv_summed(b, i - 1))
                    dve.wait_ge(*halo_out(b, i + 1 - NG))
                    if i > 0:
                        dve.wait_ge(*halo_out(b, i))
                    dve.tensor_copy(h[:, s, 0:PAD], halo[:, i, :]).then_inc(halo_in.sem, 1)
                    dve.wait_ge(*chunk_done(b, j + 1))
                    dve.wait_ge(*tmp_full(b, n + 1))
                    dve.scalar_tensor_tensor(h[:, s, PAD:PAD + B], src, bias, gated[:, n % 2, :],
                                             ALU.add, ALU.mult).then_inc(tmp_used.sem, 1)
                    dve.wait_ge(*tmp_used(b, n + 1))
                    dve.tensor_copy(halo[:, i, :], h[:, s, B:B + PAD]).then_inc(halo_out.sem, 1)
                elif kind == "u":
                    n = tmp_of[order[j]]
                    dve.wait_ge(*tmp_full(b, n + 1))
                    dve.wait_ge(*mix_gated(b, i + 1))
                    dve.tensor_tensor(y[:, NG + i, :], y[:, NG + i, :], gated[:, n % 2, :],
                                      ALU.mult).then_inc(tmp_used.sem, 1)
                elif kind == "q":
                    dve.wait_ge(*q_hi_ready(b, i + 1))
                    dve.scalar_tensor_tensor(q_part(1, i), src, bias, q_part(0, i).bitcast(F32),
                                             ALU.add, ALU.subtract).then_inc(q_split.sem, 1)

            def tap(b, g, k):
                if k == TAPS:
                    dve.wait_ge(*tap_done(b, TAPS * (g + 1)))
                    dve.tensor_tensor(y[:, g, :], acc[1], even_sum[:], ALU.add).then_inc(conv_summed.sem, 1)
                    return
                src, w = h[:, g % 2, k:k + B], cw[:, g, k:k + 1]
                if k == 0:
                    dve.wait_ge(*tmp_used(b, tmp_of[("glu", g)] + 1))
                    dve.wait_ge(*conv_summed(b, g))
                    if g == 0:
                        dve.wait_ge(*res_summed(b, 0))
                    dve.tensor_scalar(acc[0], src, w, vec_col(CONV_B, g), ALU.mult, ALU.add).then_inc(tap_done.sem, 1)
                elif k == 1:
                    dve.tensor_scalar(acc[1], src, w, None, ALU.mult).then_inc(tap_done.sem, 1)
                else:
                    dve.wait_ge(*tap_done(b, TAPS * g + k - 1))
                    dve.scalar_tensor_tensor(even_sum[:] if k == TAPS - 1 else acc[k % 2], src, w,
                                             acc[k % 2], ALU.mult, ALU.add).then_inc(tap_done.sem, 1)

            def statistics(b, n, parts):
                for k, part in enumerate(parts):
                    dve.bn_stats(bn[:, n, k, :], part).then_inc(ln_stats.sem, 1)

            def moments(b, n):
                dve.wait_ge(*ln_stats(b, 2 * n + 2))
                dve.memset(ve[:, n:n + 1], EPS)
                dve.bn_aggr(mv[:, n, :], bn[:, n, :, :]).then_inc(ln_mean.sem, 1)
                dve.wait_ge(*ln_mean(b, n + 1))
                dve.tensor_tensor(ve[:, n:n + 1], ve[:, n:n + 1], mv[:, n, 1:2], ALU.add).then_inc(ln_var.sem, 1)

            def side_stage(b, kind, i):
                src = pair_of(kind, i)
                if kind in ("v_turn", "c_turn"):
                    n = (LN_V if kind == "v_turn" else LN_C) + i
                    dve.wait_ge(*(v_turned if kind == "v_turn" else c_turned)(b, i + 1))
                    statistics(b, n, (src[:, 0, 0:C2], src[:, 1, 0:C2]))
                    moments(b, n)
                elif kind == "mix":
                    dve.wait_ge(*mixed(b, i + 1))
                    for k, hd in enumerate((2 * i, 2 * i + 1)):
                        dve.scalar_tensor_tensor(
                            src[:, k, :].rearrange("p (t s) -> p t s", t=T),
                            src[:, k, :].rearrange("p (t s) -> p t s", t=T), vec_col(GMLP_G, hd),
                            mix_bias[:, hd:hd + 1, :].to_broadcast([P, T, P]),
                            ALU.mult, ALU.add).then_inc(mix_scaled.sem, 1)
                        dve.wait_ge(*mix_scaled(b, hd + 1))
                        dve.wait_ge(*gate_ready(b, gate_of[("gmlp_gate", hd)] + 1))
                        dve.tensor_tensor(y[:, NG + hd, :], src[:, k, :], y[:, NG + hd, :],
                                          ALU.mult).then_inc(mix_gated.sem, 1)
                elif kind == "score":
                    dve.wait_ge(*scored(b, i + 1))
                    dve.tensor_reduce(mx[:, i, :], src.rearrange("p a (t m) -> p (a t) m", t=2), AX.X,
                                      ALU.max).then_inc(max_ready.sem, 1)
                    dve.wait_ge(*max_ready(b, i + 1))
                    dve.tensor_scalar(nmx[:, i, :], mx[:, i, :], -SCALE, None, ALU.mult).then_inc(nmax_ready.sem, 1)
                elif kind == "p_turn":
                    dve.wait_ge(*p_hi_ready(b, i + 1))
                    dve.tensor_tensor(p_part(1, i), src, p_part(0, i).bitcast(F32),
                                      ALU.subtract).then_inc(p_split.sem, 1)
                elif kind == "attend":
                    dve.wait_ge(*pv_done(b, i + 1))
                    dve.wait_ge(*gate_ready(b, gate_of[("x_gate", i)] + 1))
                    dve.tensor_tensor(y[:, NG + NH + i, :], src[:, 0, :], y[:, NG + NH + i, :],
                                      ALU.mult).then_inc(attended.sem, 1)
                elif kind == "c_back":
                    for c in (2 * i, 2 * i + 1):
                        dve.wait_ge(*gate_ready(b, gate_of[("conv_gate", c)] + 1))
                        dve.wait_ge(*tmp_full(b, tmp_of[("silu", c)] + 1))
                        dve.tensor_tensor(y[:, c, :], y[:, c, :], gated[:, tmp_of[("silu", c)] % 2, :],
                                          ALU.mult).then_inc(tmp_used.sem, 1)

            def softmax_end(b, i):
                dve.wait_ge(*exp_done(b, i + 1))
                dve.reciprocal(inv[:, i, :], sums[:, i, :]).then_inc(inv_ready.sem, 1)
                dve.wait_ge(*inv_ready(b, i + 1))
                dve.tensor_tensor(probs(i), probs(i),
                                  inv[:, i, :].rearrange("p (t o) -> p t o", o=1).to_broadcast([P, T, MEM]),
                                  ALU.mult).then_inc(p_ready.sem, 1)

            def normalise(b, kind, i):
                src = pair_of(kind, i)[:, :, 0:C2]
                n = (LN_V if kind == "v_turn" else LN_C) + i
                dst = v_tmp if kind == "v_turn" else c_norm(i)
                done = v_normed if kind == "v_turn" else c_normed
                dve.wait_ge(*ln_rstd(b, n + 1))
                if kind == "v_turn" and i > 0:
                    dve.wait_ge(*vn_split(b, i))
                dve.tensor_scalar(dst.rearrange("p (n c) -> p n c", n=2), src, mv[:, n, 0:1],
                                  rstd[:, n:n + 1], ALU.subtract, ALU.mult).then_inc(done.sem, 1)

            dve.memset(halo[:], 0.0).then_inc(halo_out.sem, 1)
            dve.memset(ones.bitcast(F32), 1.0)
            dve.wait_ge(vec_turned.sem, 1)
            dve.tensor_copy(cw[:].rearrange("p g k -> p (g k)"), PS[:, 5, 0:NG * TAPS]).then_inc(vec_ready.sem, 1)
            dve.tensor_copy(cols[:], PS[:, 4, 0:NV]).then_inc(vec_ready.sem, 1)
            for i in range(MC):
                dve.wait_ge(mem_hi.sem, i + 1)
                dve.tensor_tensor(x_lo[:, :, i * P:(i + 1) * P],
                                  PS[:, 2 * i:2 * i + 2, :].rearrange("p a (k s) -> p (a k) s", s=P),
                                  x_hi[:, :, i * P:(i + 1) * P].bitcast(F32), ALU.subtract).then_inc(mem_split.sem, 1)
            dve.wait_ge(ws_hi.sem, 1)
            dve.tensor_tensor(wst[:, 1, :, :].rearrange("p (n h) s -> p n (h s)", n=2), PS[:, 6:8, 0:C2],
                              wst[:, 0, :, :].rearrange("p (n h) s -> p n (h s)", n=2).bitcast(F32),
                              ALU.subtract).then_inc(ws_split.sem, 1)
            dve.wait_ge(vec_ready.sem, 2)
            for c in range(NX):
                dve.wait_ge(kv_hi.sem, c + 1)
                dve.scalar_tensor_tensor(kt[:, 1, c, :], PS[:, 4 + c % 2, 0:MEM], b_kv_col(c),
                                         kt[:, 0, c, :].bitcast(F32), ALU.add, ALU.subtract).then_inc(k_split.sem, 1)
            dve.wait_ge(row_sum.sem, 1)
            dve.wait_ge(rows_landed.sem, 4 * 16)
            for hd in range(NH):
                dve.scalar_tensor_tensor(mix_bias[:, hd, :], PS[:, 6 + hd // 3, hd % 3 * P:(hd % 3 + 1) * P],
                                         vec_col(GMLP_BETA, hd), bs_bc[:, hd * P:(hd + 1) * P],
                                         ALU.mult, ALU.add).then_inc(bias_ready.sem, 1)
            dve.wait_ge(v_hi.sem, 1)
            dve.tensor_tensor(vm[:, 1, :, :], PS[:, 0:2, :], vm[:, 0, :, :].bitcast(F32),
                              ALU.subtract).then_inc(v_split.sem, 1)
            dve.wait_ge(v_split.sem, 1)
            dve.wait_ge(bias_ready.sem, NH)
            dve.wait_ge(halo_out.sem, 1)
            dve.sem_inc(halo_out.sem, NG - 1)
            dve.sem_inc(tmp_used.sem, 2)
            dve.sem_inc(conv_summed.sem, 2)
            dve.sem_inc(res_summed.sem, T)
            dve.sem_inc(credit.sem, 1)

            def y_lo(b, e):
                dve.wait_ge(*y_hi_ready(b, e + 1))
                dve.tensor_tensor(y_part(1, e), y[:, y_order[e], :], y_part(0, e).bitcast(F32),
                                  ALU.subtract).then_inc(y_split.sem, 1)

            def out_statistics(b, t):
                dve.wait_ge(*res_summed(b, t + 1))
                statistics(b, LN_O + t, (res[:, t, 0:HALF], res[:, t, HALF:D]))
                moments(b, LN_O + t)
                dve.scalar_tensor_tensor(res[:, t, :], res[:, t, :], mv[:, LN_O + t, 0:1], lng_bc[:],
                                         ALU.subtract, ALU.mult).then_inc(ln_scaled.sem, 1)

            def out_normalise(b, t):
                dve.wait_ge(*ln_scaled(b, t + 1))
                dve.wait_ge(*ln_rstd(b, LN_O + t + 1))
                dve.scalar_tensor_tensor(res[:, t, :], res[:, t, :], rstd[:, LN_O + t:LN_O + t + 1],
                                         lnb_bc[:], ALU.mult, ALU.add).then_inc(ln_done.sem, 1)

            def step(b, j, behind=None):
                from_bank(b, j)
                taps = tap_plan.get(j, [])
                for g, k in taps[:2]:
                    tap(b, g, k)
                for kind, i in side.get(j, []):
                    side_stage(b, kind, i)
                if behind:
                    out_statistics(*behind)
                for g, k in taps[2:]:
                    tap(b, g, k)
                for kind, i in side.get(j, []):
                    if kind in ("v_turn", "c_turn"):
                        normalise(b, kind, i)
                    elif kind == "score":
                        softmax_end(b, i)
                if behind:
                    out_normalise(*behind)
                if j in y_at:
                    y_lo(b, y_at[j])

            def sum_rows(b, t):
                if t < T - 1:
                    dve.wait_ge(*out_ready(b, t + 1))
                else:
                    dve.wait_ge(*chunk_done(b, CHUNKS))
                dve.wait_ge(*res_scaled(b, t + 1))
                dve.tensor_tensor(res[:, t, :], PS[:, 2 * t:2 * t + 2, :].rearrange("p a s -> p (a s)"),
                                  res[:, t, :], ALU.add).then_inc(res_summed.sem, 1)

            def vector_block(b, last):
                for j in range(OPEN, NC_IN):
                    step(b, j)
                for e in range(YR, NC_OUT):
                    y_lo(b, e)
                    if e < YR + T:
                        t = e - YR
                        dve.wait_ge(*res_landed[t](b, 1))
                        dve.scalar_tensor_tensor(res[:, t, :], res[:, t, :], ALPHA, bout_bc[:],
                                                 ALU.mult, ALU.add).then_inc(res_scaled.sem, 1)
                if last:
                    for t in range(T):
                        sum_rows(b, t)
                        out_statistics(b, t)
                        if t > 0:
                            out_normalise(b, t - 1)
                    out_normalise(b, T - 1)
                    return
                sum_rows(b, 0)
                sum_rows(b, 1)
                x_lo_tile(b + 1, 0)
                sum_rows(b, 2)
                x_lo_tile(b + 1, 1)
                x_lo_tile(b + 1, 2)
                x_lo_tile(b + 1, 3)
                sum_rows(b, 3)
                for t in range(2):
                    out_statistics(b, t)
                    out_normalise(b, t)
                step(b + 1, 0)
                step(b + 1, 1)
                step(b + 1, 2, (b, 2))
                step(b + 1, 3, (b, 3))
                step(b + 1, 4)

            for t in range(T):
                x_lo_tile(0, t)
            for j in range(OPEN):
                step(0, j)
            with dve.Fori(0, BLOCKS - 1) as b:
                vector_block(b, False)
            vector_block(BLOCKS - 1, True)


_INS = ["x", "mem", "w_in", "b_in", "conv_w", "conv_b", "conv_ln_g", "conv_ln_b", "gmlp_ln_g",
        "gmlp_ln_b", "gmlp_ws", "gmlp_bs", "w_kv", "b_kv", "w_out", "b_out", "ln_g", "ln_b"]


def kernel(**inputs):
    import numpy as np
    import concourse.bacc as bacc
    from concourse.bass_utils import run_bass_kernel_spmd

    nc = bacc.Bacc("TRN2", target_bir_lowering=False, num_devices=1)
    arrays, args = {}, []
    for name in _INS:
        a = np.ascontiguousarray(inputs[name])
        arrays[f"in_{name}"] = a
        args.append(nc.dram_tensor(f"in_{name}", a.shape, mybir.dt.from_np(a.dtype), kind="ExternalInput").ap())
    shape = arrays["in_x"].shape
    out = nc.dram_tensor("out_y", shape, F32, kind="ExternalOutput").ap()
    layer(nc, *args, out)
    r = run_bass_kernel_spmd(nc, [arrays], core_ids=[0])
    return r.results[0]["out_y"]
```

```python
from contextlib import ExitStack

import concourse.bass as bass
from concourse import mybir

P = 128
F32 = mybir.dt.float32
F32R = mybir.dt.float32r
ACT = mybir.ActivationFunctionType
ALU = mybir.AluOpType
AX = mybir.AxisListType


class Signal:

    def __init__(self, sem, per, lead=0, unit=1):
        self.sem, self.per, self.lead, self.unit = sem, per, lead, unit

    def __call__(self, b, n):
        return self.sem, b * (self.per * self.unit) + (self.lead + n) * self.unit


def layer(nc, x, mem, w_in, b_in, conv_w, conv_b, conv_ln_g, conv_ln_b, gmlp_ln_g, gmlp_ln_b,
          gmlp_ws, gmlp_bs, w_kv, b_kv, w_out, b_out, ln_g, ln_b, out):
    _, S, D = x.shape
    MEM = mem.shape[1]
    E_IN = w_in.shape[2]
    TAPS = conv_w.shape[1]
    DC = conv_w.shape[2]
    E_OUT = w_out.shape[1]
    DX = w_kv.shape[2] // 2
    KD = D // P
    NG = DC // P
    NH = gmlp_ws.shape[1]
    NX = DX // P
    MC = MEM // P
    B = 512
    T = B // P
    BLOCKS = S // B
    HALF = 512
    NC_IN = E_IN // P
    NC_OUT = E_OUT // P
    CHUNKS = NC_IN + NC_OUT
    KV = 2 * NX
    WR = 3
    PAD = TAPS - 1
    ALPHA = 2.0 ** 0.25
    EPS = 1e-5
    SCALE = float(P) ** -0.5
    C2 = DC // 2
    assert NG == 6 and NH == 6 and NX == 4 and KD == 8 and T == 4 and MC == 2 and D == 2 * HALF
    assert CHUNKS % WR == 0 and BLOCKS * B == S and DX == HALF

    order = []
    others = ([("v", c) for c in range(6)] + [("gmlp_gate", c) for c in range(6)]
              + [("q", c) for c in range(4)] + [("x_gate", c) for c in range(2)])
    for g in range(NG):
        order += [("glu", g), ("a", g)] + others[3 * g:3 * g + 3]
    order += [("x_gate", 2), ("x_gate", 3)] + [("u", c) for c in range(6)]
    order += [("conv_gate", c) for c in range(6)]
    assert len(order) == NC_IN
    first = {"a": 0, "glu": 6, "conv_gate": 12, "u": 18, "v": 24, "gmlp_gate": 30, "q": 36,
             "x_gate": 40}
    y_order = list(range(6, 16)) + list(range(6))
    side = {10: [("v_turn", 0)], 11: [("v_turn", 1)], 12: [("v_turn", 2)], 13: [("v_turn", 3)],
            16: [("mix", 0)], 17: [("mix", 1)], 18: [("mix", 2)], 19: [("mix", 3)],
            20: [("mix", 4)], 21: [("mix", 5)],
            23: [("score", 0)], 24: [("score", 1)], 26: [("p_turn", 0)],
            27: [("p_turn", 1), ("score", 2)], 28: [("score", 3)], 29: [("attend", 0)],
            30: [("attend", 1), ("p_turn", 2)], 31: [("p_turn", 3)], 32: [("attend", 2)], 33: [("attend", 3)],
            34: [("c_turn", 0), ("c_turn", 1)], 35: [("c_turn", 2), ("c_turn", 3)],
            37: [("c_spread", 0)]}
    PAIR_USES = [("x_turn", t) for t in range(T)]
    for j in range(NC_IN):
        PAIR_USES += side.get(j, [])
    PAIR_USES += [("idle", 0), ("out", 0), ("out", 1)]
    assert len(PAIR_USES) % 2 == 0
    y_at = {38: 0, 39: 1, 40: 2, 41: 3}
    YR = 4
    OPEN = 5
    use_of = {k: u for u, k in enumerate(PAIR_USES)}
    tmp_uses = []
    for j in range(NC_IN):
        if order[j][0] in ("glu", "u"):
            tmp_uses.append(order[j])
        elif order[j][0] == "conv_gate":
            tmp_uses.append(("silu", order[j][1]))
    tmp_of = {k: i for i, k in enumerate(tmp_uses)}
    gate_of = {k: i for i, k in enumerate([o for o in order if "gate" in o[0]])}
    N_TMP = len(tmp_uses)
    LN_V, LN_C, LN_O = 0, T, 2 * T
    N_LN = 3 * T
    TAP_OPS = TAPS + 1
    tap_plan = {}
    for g in range(NG):
        n = 0
        for s, k in enumerate([7, 7, 6, 6, 6]):
            tap_plan[5 * g + 2 + s] = [(g, n + i) for i in range(k)]
            n += k
        assert n == TAP_OPS

    ctx = ExitStack()
    with ctx:
        def sb(name, shape, dt=F32):
            return ctx.enter_context(nc.sbuf_tensor(name, shape, dt))

        def signal(name, per=0, lead=0, unit=1):
            return Signal(ctx.enter_context(nc.semaphore(name)), per, lead, unit)

        PS = ctx.enter_context(nc.psum_tensor("banks", [P, 8, HALF], F32))
        x_hi = sb("x_hi", [P, KD, B], F32R)
        x_lo = sb("x_lo", [P, KD, B], F32R)
        whl = sb("w_split", [P, WR, 2, KD * P], F32R)
        kt = sb("k_split", [P, 2, NX, MEM], F32R)
        vm = sb("v_split", [P, 2, MC, DX], F32R)
        wst = sb("ws_split", [P, 2, NH, P], F32R)
        side_r = sb("side_split", [P, 2 * T * DC], F32R)
        wstage = sb("w_stage", [P, WR, KD * P])
        work = sb("work", [P, T * D])
        res = sb("residual", [P, T, D])
        y = sb("y_t", [P, NC_OUT, B])
        gated = sb("gated", [P, 2, B])
        h = sb("conv_in", [P, 2, PAD + B])
        halo = sb("halo", [P, NG, PAD])
        even_sum = sb("even_sum", [P, B])
        ident = sb("ident", [P, P])
        mix_bias = sb("mix_bias", [P, NH, P])
        bout_bc = sb("b_out_rows", [P, D])
        lng_bc = sb("ln_g_rows", [P, D])
        lnb_bc = sb("ln_b_rows", [P, D])
        NV = NC_IN + KV + 5 * NG
        cols = sb("vector_columns", [P, NV])
        cw = sb("conv_w_columns", [P, NG, TAPS])
        neg_half = sb("neg_half", [P, 1])
        bn = sb("bn", [P, N_LN, 2, 6])
        mv = sb("mean_var", [P, N_LN, 2])
        ve = sb("var_eps", [P, N_LN])
        rstd = sb("rstd", [P, N_LN])
        mx = sb("score_max", [P, NX, T])
        nmx = sb("neg_max", [P, NX, T])
        sums = sb("exp_sums", [P, NX, T])
        inv = sb("inv_sums", [P, NX, T])

        yf = y[:].rearrange("p c s -> p (c s)")
        cw_nat = yf[0:TAPS, 0:DC]
        ws_nat = yf[:, DC:2 * DC].rearrange("p (h s) -> p h s", h=NH)
        ws_low = yf[:, 2 * DC:3 * DC].rearrange("p (h s) -> p h s", h=NH)
        bs_bc = yf[:, 3 * DC:4 * DC]
        vec_nat = yf[0:NV, 4 * DC:4 * DC + P]
        vec_rows = lambda k: vec_nat[NC_IN + KV + k * NG:NC_IN + KV + (k + 1) * NG, :]
        vt_nat = yf[:, 8 * HALF:8 * HALF + NX * MEM].rearrange("p (h m) -> p h m", h=NX)
        mem_part = lambda part: side_r[:, part * KD * MEM:(part + 1) * KD * MEM].rearrange(
            "p (k m) -> p k m", k=KD)
        ones = side_r[:, 2 * KD * MEM:2 * KD * MEM + P]

        b_in_col = lambda c: cols[:, c:c + 1]
        b_kv_col = lambda c: cols[:, NC_IN + c:NC_IN + c + 1]
        vec_col = lambda k, c: cols[:, NC_IN + KV + k * NG + c:NC_IN + KV + k * NG + c + 1]
        CONV_B, CONV_G, CONV_BETA, GMLP_G, GMLP_BETA = range(5)

        def v_norm(part, t):
            return side_r[:, (part * T + t) * DC:(part * T + t + 1) * DC]

        def q_part(part, hd):
            return side_r[:, (hd % 2 * 2 + part) * B:(hd % 2 * 2 + part + 1) * B]

        def p_part(part, hd):
            at = 4 * B + (hd % 2 * 2 + part) * MC * B
            return side_r[:, at:at + MC * B].rearrange("p (c s) -> p c s", c=MC)

        def y_part(part, e):
            at = 4 * B + (e % YR * 2 + part) * B
            return side_r[:, at:at + B]

        x_tile = lambda t: work[:, t * D:(t + 1) * D]
        v_act = lambda c: work[:, c * B:(c + 1) * B]
        v_tmp = work[:, NH * B:NH * B + DC]
        probs = lambda hd: work[:, hd % 2 * T * MEM:(hd % 2 + 1) * T * MEM].rearrange(
            "p (t m) -> p t m", t=T)
        c_norm = work[:, 0:NG * B].rearrange("p (c s) -> p c s", c=NG)
        c_wide = lambda n: work[:, (NG + n) * B:(NG + n + 1) * B].rearrange("p (t s) -> p t s", t=T)

        def pair_of(kind, i):
            p = use_of[(kind, i)] % 2
            return PS[:, 2 * p:2 * p + 2, :]

        mix_part = lambda hd: work[:, hd % 2 * B:(hd % 2 + 1) * B].rearrange("p (t s) -> p t s", t=T)

        def mix_sums(hd):
            return pair_of("mix", hd).rearrange("p a (n c s) -> p (a n) c s", n=2, c=2)

        def bank_of(j):
            return PS[:, 4 + j % 2, :]

        acc = [PS[:, 6, :], PS[:, 7, :]]

        mem_landed = [signal(f"mem_landed{i}") for i in range(MC)]
        vec_landed = signal("vectors_landed")
        ln_vec_landed = signal("ln_vectors_landed")
        ws_landed = signal("ws_landed")
        rows_landed = signal("rows_landed")
        idr = signal("identity_ready")
        msk = signal("ws_masked")
        vec_turned = signal("vectors_turned")
        vec_ready = signal("vectors_ready")
        mem_turned = signal("mem_turned")
        mem_hi = signal("mem_hi_ready")
        mem_split = signal("mem_split_ready")
        ws_turned = signal("ws_turned")
        ws_hi = signal("ws_hi_ready")
        ws_split = signal("ws_split_ready")
        row_sum = signal("ws_row_sums")
        bias_ready = signal("mix_bias_ready")
        kv_hi = signal("k_hi_or_v_ready")
        k_split = signal("k_split_ready")
        v_back = signal("v_memory_turned")
        v_hi = signal("v_memory_hi")
        v_split = signal("v_memory_split")

        w_landed = [signal(f"w_landed{s}", CHUNKS // WR, 0, 16) for s in range(WR)]
        w_hi = signal("w_hi_ready", CHUNKS, KV)
        w_split = signal("w_split_ready", CHUNKS, KV)
        chunk_done = signal("chunk_done", CHUNKS, KV)
        x_landed = [signal(f"x_landed{t}", 1, 0, 16) for t in range(T)]
        res_landed = [signal(f"residual_landed{t}", 1, 0, 16) for t in range(T)]
        stored = [signal(f"out_stored{t}", 1, 0, 16) for t in range(T)]
        x_turned = signal("x_turned", T)
        x_hi_ready = signal("x_hi_ready", T)
        x_split = signal("x_split_ready", T)
        tmp_full = signal("gated_full", N_TMP)
        tmp_used = signal("gated_used", N_TMP, 2)
        v_ready = signal("v_ready", NH)
        gate_ready = signal("gate_ready", len(gate_of))
        q_hi_ready = signal("q_hi_ready", NX)
        q_split = signal("q_split_ready", NX)
        halo_in = signal("halo_in", NG)
        halo_out = signal("halo_out", NG, NG)
        tap_done = signal("tap_done", NG * TAPS)
        conv_summed = signal("conv_summed", NG, 2)
        v_turned = signal("v_turned", T)
        v_normed = signal("v_normed", T)
        vn_hi = signal("v_norm_hi", T)
        vn_split = signal("v_norm_split", T)
        ln_stats = signal("ln_stats", 2 * N_LN)
        ln_mean = signal("ln_mean", N_LN)
        ln_var = signal("ln_var_eps", N_LN)
        ln_rstd = signal("ln_rstd", N_LN)
        mixed = signal("mixed", NH)
        mix_scaled = signal("mix_scaled", 2 * NH)
        mix_gated = signal("mix_gated", NH)
        scored = signal("scored", NX)
        max_ready = signal("max_ready", NX)
        nmax_ready = signal("neg_max_ready", NX)
        exp_done = signal("exp_done", NX)
        inv_ready = signal("inv_ready", NX)
        p_ready = signal("probs_ready", NX)
        p_turned = signal("probs_turned", NX)
        p_hi_ready = signal("probs_hi_ready", NX)
        p_split = signal("probs_split_ready", NX)
        pv_done = signal("pv_done", NX)
        attended = signal("attended", NX)
        c_turned = signal("conv_turned", T)
        c_widened = signal("conv_moments_wide", 2)
        c_spread = signal("conv_moments_spread", 1)
        c_centred = signal("conv_centred", 2)
        c_normed = signal("conv_normed", 2)
        y_hi_ready = signal("y_hi_ready", NC_OUT)
        y_split = signal("y_split_ready", NC_OUT)
        out_ready = signal("out_ready", T - 1)
        res_scaled = signal("residual_scaled", T)
        res_summed = signal("residual_summed", T, T)
        ln_scaled = signal("out_ln_scaled", T)
        ln_done = signal("out_ln_done", T)
        last_scaled = signal("last_rows_scaled")
        last_added = signal("last_rows_added")

        def bank_released(b, j):
            kind, i = order[j]
            if kind in ("glu", "u"):
                return tmp_full(b, tmp_of[order[j]] + 1)
            if kind == "a":
                return tmp_used(b, tmp_of[("glu", i)] + 1)
            if kind == "v":
                return v_ready(b, i + 1)
            if kind == "q":
                return q_split(b, i + 1)
            return gate_ready(b, gate_of[order[j]] + 1)

        def pair_released(b, u):
            kind, i = PAIR_USES[u]
            return {
                "x_turn": lambda: x_split(b, i + 1),
                "v_turn": lambda: v_normed(b, i + 1),
                "mix": lambda: mix_scaled(b, 2 * i + 2),
                "score": lambda: exp_done(b, i + 1),
                "p_turn": lambda: p_split(b, i + 1),
                "attend": lambda: attended(b, i + 1),
                "c_turn": lambda: ln_stats(b, 2 * (LN_C + i) + 2),
                "c_spread": lambda: c_normed(b, 2),
                "idle": lambda: pair_released(b, u - 2),
                "out": lambda: res_summed(b, i + 1 - T),
            }[kind]()

        def y_final(b, c):
            if c < NG:
                return tmp_used(b, tmp_of[("silu", c)] + 1)
            if c < NG + NH:
                return tmp_used(b, tmp_of[("u", c - NG)] + 1)
            return attended(b, c - NG - NH + 1)

        slot_of = lambda j: (KV + j) % WR

        x_rows = x.rearrange("o s d -> (o s) d")
        out_rows = out.rearrange("o s d -> (o s) d")
        w_in_v = w_in.rearrange("l (k p) e -> p (l k) e", p=P)
        w_kv_v = w_kv.rearrange("l (k p) e -> p (l k) e", p=P)
        w_out_v = w_out.rearrange("l e n -> (l e) n")
        mem_rows = mem.rearrange("o m d -> (o m) d")

        block = ctx.enter_context(nc.Block())

        @block.sync
        def _(sp):
            def load_w(b, j):
                s = slot_of(j)
                if not (isinstance(b, int) and b == 0 and KV + j < WR):
                    sp.wait_ge(*w_split(b, j - WR + 1))
                dst = wstage[:, s, :]
                if j < 0:
                    src = w_kv_v[:, :, (KV + j) * P:(KV + j + 1) * P]
                elif j < NC_IN:
                    kind, i = order[j]
                    c = first[kind] + i
                    src = w_in_v[:, :, c * P:(c + 1) * P]
                else:
                    c = y_order[j - NC_IN]
                    sp.dma_start(dst, w_out_v[c * P:(c + 1) * P, :]).then_inc(w_landed[s].sem, 16)
                    return
                sp.dma_start(dst.rearrange("p (k e) -> p k e", k=KD), src).then_inc(w_landed[s].sem, 16)

            def load_x(b, t):
                sp.dma_start(x_tile(t), x_rows[bass.ds(b * B + t * P, P), :]).then_inc(x_landed[t].sem, 16)

            def load_rows(b, t, behind):
                if behind:
                    sp.wait_ge(*stored[t](b, 0))
                sp.dma_start(res[:, t, :], x_rows[bass.ds(b * B + t * P, P), :]).then_inc(
                    res_landed[t].sem, 16)

            for i in range(MC):
                sp.dma_start(res[:, i, :], mem_rows[i * P:(i + 1) * P, :]).then_inc(mem_landed[i].sem, 16)
            for j in range(-KV, WR - KV):
                load_w(0, j)
            for t in range(T):
                sp.dma_start(x_tile(t), x_rows[t * P:(t + 1) * P, :]).then_inc(x_landed[t].sem, 16)
                load_w(0, WR - KV + t)
            for j in range(WR - KV + T, 0):
                load_w(0, j)

            rows_at, x_at = (24, 27, 30, 33), (47, 49, 51, 53)

            def sync_block(b, last):
                for j in range(CHUNKS):
                    load_w(b, j)
                    if j in rows_at and last:
                        load_rows(b, rows_at.index(j), True)
                    elif j in rows_at:
                        with sp.If(b > 0):
                            load_rows(b, rows_at.index(j), True)
                        with sp.Else():
                            load_rows(b, rows_at.index(j), False)
                    if j in x_at and not last:
                        if j == x_at[0]:
                            sp.wait_ge(*tmp_full(b, N_TMP))
                        load_x(b + 1, x_at.index(j))

            sp.wait_ge(mem_turned.sem, MC)
            with sp.Fori(0, BLOCKS - 1) as b:
                sync_block(b, False)
            sync_block(BLOCKS - 1, True)
            for t in range(T):
                sp.wait_ge(*stored[t](BLOCKS - 1, 1))

        @block.tensor
        def _(pe):
            def turn_x(b, t):
                pe.wait_ge(*x_landed[t](b, 1))
                pe.wait_ge(*pair_released(b, use_of[("x_turn", t)] - 2))
                dst = pair_of("x_turn", t)
                for k in range(KD):
                    m = pe.transpose(dst[:, k // 4, k % 4 * P:(k % 4 + 1) * P],
                                     x_tile(t)[:, k * P:(k + 1) * P], ident[:])
                m.then_inc(x_turned.sem, 1)

            def product(dst, w, moving_hi, moving_lo, steps, n_inc):
                for k in range(steps):
                    pe.matmul(dst, w(0, k), moving_hi(k), start=(k == 0), stop=False)
                    pe.matmul(dst, w(0, k), moving_lo(k), start=False, stop=False)
                    m = pe.matmul(dst, w(1, k), moving_hi(k), start=False, stop=(k == steps - 1))
                if n_inc is not None:
                    m.then_inc(n_inc.sem, 1)

            def project(b, j):
                s = slot_of(j)
                pe.wait_ge(*w_split(b, j + 1))
                if j < 2:
                    pe.wait_ge(*res_summed(b, 3 - T))
                else:
                    pe.wait_ge(*bank_released(b, j - 2))
                if j == 0:
                    for n in range(2):
                        pe.wait_ge(*x_split(b, 2 * n + 2))
                        at = slice(n * 2 * P, (n + 1) * 2 * P)
                        product(bank_of(j)[:, at], lambda part, k: whl[:, s, part, k * P:(k + 1) * P],
                                lambda k: x_hi[:, k, at], lambda k: x_lo[:, k, at], KD,
                                chunk_done if n == 1 else None)
                    return
                product(bank_of(j), lambda part, k: whl[:, s, part, k * P:(k + 1) * P],
                        lambda k: x_hi[:, k, :], lambda k: x_lo[:, k, :], KD, chunk_done)

            def side_stage(b, kind, i):
                pe.wait_ge(*pair_released(b, use_of[(kind, i)] - 2))
                dst = pair_of(kind, i)
                if kind == "v_turn":
                    pe.wait_ge(*v_ready(b, NH))
                    for c in range(NH):
                        m = pe.transpose(dst[:, c // 3, c % 3 * P:(c % 3 + 1) * P],
                                         v_act(c)[:, i * P:(i + 1) * P], ident[:])
                    m.then_inc(v_turned.sem, 1)
                elif kind == "mix":
                    pe.wait_ge(*vn_split(b, T))
                    for t in range(T):
                        d = mix_sums(i)[:, t, :, :]
                        vh = v_norm(0, t)[:, i * P:(i + 1) * P]
                        vl = v_norm(1, t)[:, i * P:(i + 1) * P]
                        pe.matmul(d, vh, wst[:, :, i, :], start=True, stop=False)
                        m = pe.matmul(d[:, 0, :], vl, wst[:, 0, i, :], start=False, stop=True)
                    m.then_inc(mixed.sem, 1)
                elif kind == "score":
                    pe.wait_ge(*q_split(b, i + 1))
                    for t in range(T):
                        d = dst[:, t // 2, t % 2 * MEM:(t % 2 + 1) * MEM]
                        qh = q_part(0, i)[:, t * P:(t + 1) * P]
                        ql = q_part(1, i)[:, t * P:(t + 1) * P]
                        pe.matmul(d, qh, kt[:, 0, i, :], start=True, stop=False)
                        pe.matmul(d, qh, kt[:, 1, i, :], start=False, stop=False)
                        m = pe.matmul(d, ql, kt[:, 0, i, :], start=False, stop=True)
                    m.then_inc(scored.sem, 1)
                elif kind == "p_turn":
                    pe.wait_ge(*p_ready(b, i + 1))
                    for c in range(MC):
                        for t in range(T):
                            m = pe.transpose(dst[:, c, t * P:(t + 1) * P],
                                             probs(i)[:, t, c * P:(c + 1) * P], ident[:])
                    m.then_inc(p_turned.sem, 1)
                elif kind == "attend":
                    pe.wait_ge(*p_split(b, i + 1))
                    product(dst[:, 0, :], lambda part, k: vm[:, part, k, i * P:(i + 1) * P],
                            lambda k: p_part(0, i)[:, k, :], lambda k: p_part(1, i)[:, k, :],
                            MC, pv_done)
                elif kind == "c_turn":
                    pe.wait_ge(*conv_summed(b, NG))
                    for c in range(NG):
                        m = pe.transpose(dst[:, c // 3, c % 3 * P:(c % 3 + 1) * P],
                                         y[:, c, i * P:(i + 1) * P], ident[:])
                    m.then_inc(c_turned.sem, 1)
                elif kind == "c_spread":
                    for n in range(2):
                        pe.wait_ge(*c_widened(b, n + 1))
                        for t in range(T):
                            m = pe.transpose(dst[:, n, t * P:(t + 1) * P], c_wide(n)[:, t, :], ident[:])
                    m.then_inc(c_spread.sem, 1)

            def project_out(b, e, t):
                s = slot_of(NC_IN + e)
                yh = y_part(0, e)[:, t * P:(t + 1) * P]
                yl = y_part(1, e)[:, t * P:(t + 1) * P]
                for n in range(2):
                    d = PS[:, 2 * t + n, :]
                    wh = whl[:, s, 0, n * HALF:(n + 1) * HALF]
                    wl = whl[:, s, 1, n * HALF:(n + 1) * HALF]
                    pe.matmul(d, yh, wh, start=(e == 0), stop=False)
                    pe.matmul(d, yh, wl, start=False, stop=False)
                    m = pe.matmul(d, yl, wh, start=False, stop=(e == NC_OUT - 1))
                return m

            pe.wait_ge(idr.sem, 2)
            for i in range(MC):
                pe.wait_ge(mem_landed[i].sem, 16)
                for k in range(KD):
                    m = pe.transpose(PS[:, 2 * i + k // 4, k % 4 * P:(k % 4 + 1) * P],
                                     res[:, i, k * P:(k + 1) * P], ident[:])
                m.then_inc(mem_turned.sem, 1)
            pe.wait_ge(vec_landed.sem, 5 * 16)
            pe.wait_ge(ln_vec_landed.sem, 3 * 16)
            pe.transpose(PS[:, 6, 0:NV], vec_nat, ident[0:NV, 0:NV])
            for g in range(NG):
                m = pe.transpose(PS[:, 7, g * TAPS:(g + 1) * TAPS], cw_nat[:, g * P:(g + 1) * P],
                                 ident[0:TAPS, 0:TAPS])
            m.then_inc(vec_turned.sem, 1)
            pe.wait_ge(mem_split.sem, MC)
            for c in range(KV):
                pe.wait_ge(*w_split(0, c - KV + 1))
                if c >= 2:
                    if c - 2 < NX:
                        pe.wait_ge(k_split.sem, c - 1)
                    else:
                        pe.wait_ge(kv_hi.sem, c - 1)
                s = c % WR
                product(PS[:, 4 + c % 2, 0:MEM], lambda part, k: whl[:, s, part, k * P:(k + 1) * P],
                        lambda k: mem_part(0)[:, k, :], lambda k: mem_part(1)[:, k, :], KD, chunk_done)
                if c == 1:
                    pe.wait_ge(vec_ready.sem, 2)
                    pe.wait_ge(msk.sem, 1)
                    for hd in range(NH):
                        m = pe.transpose(PS[:, 6 + hd // 3, hd % 3 * P:(hd % 3 + 1) * P],
                                         ws_low[:, hd, :], ident[:])
                    m.then_inc(ws_turned.sem, 1)
                elif c < 2 + T:
                    if c >= 2:
                        turn_x(0, c - 2)
                elif c == 2 + T:
                    pe.wait_ge(ws_split.sem, 1)
                    for n in range(2):
                        for part in range(2):
                            m = pe.matmul(PS[:, 6 + n, 0:C2], ones,
                                          wst[:, part, 3 * n:3 * n + 3, :], start=(part == 0), stop=(part == 1))
                    m.then_inc(row_sum.sem, 1)
            pe.wait_ge(kv_hi.sem, KV)
            pe.wait_ge(*x_split(0, T))
            for c in range(MC):
                for hd in range(NX):
                    m = pe.transpose(PS[:, c, hd * P:(hd + 1) * P], vt_nat[:, hd, c * P:(c + 1) * P],
                                     ident[:])
            m.then_inc(v_back.sem, 1)

            def tensor_block(b, last):
                for j in range(1, NC_IN):
                    project(b, j)
                    for kind, i in side.get(j, []):
                        side_stage(b, kind, i)
                late = 3 if last else 2
                for e in range(NC_OUT - late):
                    pe.wait_ge(*w_split(b, NC_IN + e + 1))
                    pe.wait_ge(*y_split(b, e + 1))
                    for t in range(T):
                        if e == 0 and t < 2:
                            pe.wait_ge(*pair_released(b, use_of[("out", t)] - 2))
                        elif e == 0 and t == 2:
                            pe.wait_ge(*bank_released(b, NC_IN - 2))
                            pe.wait_ge(*bank_released(b, NC_IN - 1))
                        elif e == 0:
                            pe.wait_ge(*conv_summed(b, NG))
                        m = project_out(b, e, t)
                    m.then_inc(chunk_done.sem, 1)
                for t in range(T):
                    for e in range(NC_OUT - late, NC_OUT):
                        if t == 0:
                            pe.wait_ge(*w_split(b, NC_IN + e + 1))
                            pe.wait_ge(*y_split(b, e + 1))
                        m = project_out(b, e, t)
                        if t == T - 1:
                            m.then_inc(chunk_done.sem, 1)
                            if e == NC_OUT - 2 and not last:
                                turn_x(b + 1, T - 2)
                    if t < T - 1:
                        m.then_inc(out_ready.sem, 1)
                    if 0 < t < T - 1 and not last:
                        turn_x(b + 1, t - 1)
                if not last:
                    turn_x(b + 1, T - 1)
                    project(b + 1, 0)

            project(0, 0)
            pe.wait_ge(v_split.sem, 1)
            with pe.Fori(0, BLOCKS - 1) as b:
                tensor_block(b, False)
            tensor_block(BLOCKS - 1, True)

        @block.scalar
        def _(act):
            def weight_hi(b, j):
                s = slot_of(j)
                n = (KV + j) // WR + 1
                act.wait_ge(w_landed[s].sem, b * (16 * (CHUNKS // WR)) + 16 * n)
                if not (isinstance(b, int) and b == 0 and KV + j < WR):
                    act.wait_ge(*chunk_done(b, j - WR + 1))
                act.copy(whl[:, s, 0, :], wstage[:, s, :]).then_inc(w_hi.sem, 1)

            def x_hi_tile(b, t):
                act.wait_ge(*x_turned(b, t + 1))
                act.copy(x_hi[:, :, t * P:(t + 1) * P],
                         pair_of("x_turn", t).rearrange("p a (k s) -> p (a k) s", s=P)).then_inc(
                    x_hi_ready.sem, 1)

            def from_bank(b, j):
                kind, i = order[j]
                src, bias = bank_of(j), b_in_col(first[kind] + i)
                if kind == "a":
                    return
                act.wait_ge(*chunk_done(b, j + 1))
                if kind in ("glu", "u"):
                    n = tmp_of[order[j]]
                    act.wait_ge(*tmp_used(b, n - 1))
                    act.activation(gated[:, n % 2, :], src,
                                   ACT.Sigmoid if kind == "glu" else ACT.Gelu_apprx_tanh,
                                   bias=bias).then_inc(tmp_full.sem, 1)
                elif kind == "v":
                    act.activation(v_act(i), src, ACT.Gelu_apprx_tanh, bias=bias).then_inc(v_ready.sem, 1)
                elif kind == "q":
                    act.activation(q_part(0, i), src, ACT.Identity, bias=bias).then_inc(q_hi_ready.sem, 1)
                else:
                    c = {"conv_gate": 0, "gmlp_gate": NG, "x_gate": NG + NH}[kind] + i
                    if kind == "conv_gate":
                        act.wait_ge(*c_centred(b, i // 3 + 1))
                    act.activation(y[:, c, :], src, ACT.Silu, bias=bias).then_inc(gate_ready.sem, 1)
                    if kind == "conv_gate":
                        k = tmp_of[("silu", i)]
                        act.wait_ge(*c_normed(b, i // 3 + 1))
                        act.wait_ge(*tmp_used(b, k - 1))
                        act.activation(gated[:, k % 2, :], c_norm[:, i, :], ACT.Silu,
                                       bias=vec_col(CONV_BETA, i), scale=vec_col(CONV_G, i)).then_inc(
                            tmp_full.sem, 1)

            def v_norm_hi(b, i):
                act.wait_ge(*v_normed(b, i + 1))
                act.copy(v_norm(0, i), v_tmp).then_inc(vn_hi.sem, 1)

            def side_stage(b, kind, i):
                if kind == "score":
                    act.wait_ge(*scored(b, i + 1))
                    act.wait_ge(*nmax_ready(b, i + 1))
                    if i == 0:
                        act.wait_ge(*mix_gated(b, NH))
                    for t in range(T):
                        m = act.activation(probs(i)[:, t, :],
                                           pair_of(kind, i)[:, t // 2, t % 2 * MEM:(t % 2 + 1) * MEM],
                                           ACT.Exp, bias=nmx[:, i, t:t + 1], scale=SCALE,
                                           accum_out=sums[:, i, t:t + 1])
                    m.then_inc(exp_done.sem, 1)
                elif kind == "p_turn":
                    act.wait_ge(*p_turned(b, i + 1))
                    act.copy(p_part(0, i), pair_of(kind, i)).then_inc(p_hi_ready.sem, 1)

            def y_hi(b, e):
                if e >= YR:
                    act.wait_ge(*chunk_done(b, NC_IN + e - YR + 1))
                act.wait_ge(*y_final(b, y_order[e]))
                act.copy(y_part(0, e), y[:, y_order[e], :]).then_inc(y_hi_ready.sem, 1)

            act.dma_start(vec_nat[0:NC_IN, :], b_in.rearrange("l (r c) -> (l r) c", c=P)).then_inc(vec_landed.sem, 16)
            act.dma_start(vec_nat[NC_IN:NC_IN + KV, :], b_kv.rearrange("l (r c) -> (l r) c", c=P)).then_inc(vec_landed.sem, 16)
            act.dma_start(cw_nat, conv_w.rearrange("l k c -> (l k) c")).then_inc(vec_landed.sem, 16)
            for k, v in enumerate((conv_b, conv_ln_g)):
                act.dma_start(vec_rows(k), v.rearrange("l (r c) -> (l r) c", c=P)).then_inc(vec_landed.sem, 16)
            for i in range(MC):
                act.wait_ge(mem_turned.sem, i + 1)
                act.copy(mem_part(0)[:, :, i * P:(i + 1) * P],
                         PS[:, 2 * i:2 * i + 2, :].rearrange("p a (k s) -> p (a k) s", s=P)).then_inc(mem_hi.sem, 1)
                weight_hi(0, i - KV)
            weight_hi(0, 2 - KV)
            act.wait_ge(vec_ready.sem, 2)
            for c in range(KV):
                act.wait_ge(*chunk_done(0, c - KV + 1))
                src = PS[:, 4 + c % 2, 0:MEM]
                dst = kt[:, 0, c, :] if c < NX else vt_nat[:, c - NX, :]
                act.activation(dst, src, ACT.Identity, bias=b_kv_col(c)).then_inc(kv_hi.sem, 1)
                weight_hi(0, c + WR - KV)
                if c == 1:
                    act.wait_ge(ws_turned.sem, 1)
                    act.copy(wst[:, 0, :, :].rearrange("p (n h) s -> p n (h s)", n=2), PS[:, 6:8, 0:C2]).then_inc(ws_hi.sem, 1)
                elif 2 <= c < 2 + T:
                    x_hi_tile(0, c - 2)
            act.wait_ge(v_back.sem, 1)
            act.copy(vm[:, 0, :, :], PS[:, 0:2, :]).then_inc(v_hi.sem, 1)

            def scalar_block(b, last):
                for j in range(NC_IN):
                    from_bank(b, j)
                    weight_hi(b, j + WR)
                    for kind, i in side.get(j - 1, []):
                        if kind == "v_turn":
                            v_norm_hi(b, i)
                    for kind, i in side.get(j, []):
                        side_stage(b, kind, i)
                    if j in y_at:
                        y_hi(b, y_at[j])
                for e in range(NC_OUT):
                    if NC_IN + e + WR < CHUNKS:
                        weight_hi(b, NC_IN + e + WR)
                    if e + YR < NC_OUT:
                        y_hi(b, e + YR)
                if not last:
                    weight_hi(b, CHUNKS)
                    x_hi_tile(b + 1, 0)
                    x_hi_tile(b + 1, 1)
                    x_hi_tile(b + 1, 2)
                    weight_hi(b, CHUNKS + 1)
                    x_hi_tile(b + 1, 3)
                    weight_hi(b, CHUNKS + 2)
                else:
                    for t in range(T - 1):
                        act.wait_ge(*ln_scaled(b, t + 1))
                        act.wait_ge(*ln_rstd(b, LN_O + t + 1))
                        act.activation(res[:, t, :], res[:, t, :], ACT.Identity,
                                       scale=rstd[:, LN_O + t:LN_O + t + 1]).then_inc(last_scaled.sem, 1)

            with act.Fori(0, BLOCKS - 1) as b:
                scalar_block(b, False)
            scalar_block(BLOCKS - 1, True)

        @block.gpsimd
        def _(pool):
            def weight_lo(b, j):
                s = slot_of(j)
                pool.wait_ge(*w_hi(b, j + 1))
                pool.tensor_tensor(whl[:, s, 1, :], wstage[:, s, :], whl[:, s, 0, :].bitcast(F32),
                                   ALU.subtract).then_inc(w_split.sem, 1)

            def inv_std(b, n):
                pool.wait_ge(*ln_var(b, n + 1))
                pool.tensor_tensor(rstd[:, n:n + 1], ve[:, n:n + 1], neg_half[:], ALU.pow).then_inc(ln_rstd.sem, 1)

            def side_stage(b, kind, i):
                if kind == "v_turn":
                    inv_std(b, LN_V + i)
                elif kind == "c_turn":
                    inv_std(b, LN_C + i)

            def v_norm_lo(b, i):
                pool.wait_ge(*vn_hi(b, i + 1))
                pool.tensor_tensor(v_norm(1, i), v_tmp, v_norm(0, i).bitcast(F32),
                                   ALU.subtract).then_inc(vn_split.sem, 1)

            def mix_gate(b, i):
                pool.wait_ge(*mix_scaled(b, 2 * i + 2))
                pool.wait_ge(*gate_ready(b, gate_of[("gmlp_gate", i)] + 1))
                gate = y[:, NG + i, :].rearrange("p (t s) -> p t s", t=T)
                pool.tensor_tensor(gate, mix_part(i), gate, ALU.mult).then_inc(mix_gated.sem, 1)

            def softmax_end(b, i):
                pool.wait_ge(*exp_done(b, i + 1))
                pool.wait_ge(*inv_ready(b, i + 1))
                pool.tensor_tensor(probs(i), probs(i),
                                   inv[:, i, :].rearrange("p (t o) -> p t o", o=1).to_broadcast([P, T, MEM]),
                                   ALU.mult).then_inc(p_ready.sem, 1)

            def await_rows(b, t):
                pool.wait_ge(*ln_done(b, t + 1))

            def store(b, t):
                pool.dma_start(out_rows[bass.ds(b * B + t * P, P), :],
                               res[:, t, :]).then_inc(stored[t].sem, 16)

            pool.memset(ident[:], 0.0).then_inc(idr.sem, 1)
            pool.memset(neg_half[:], -0.5)
            pool.wait_ge(idr.sem, 1)
            pool.affine_select(out=ident[:], in_=ident[:], compare_op=ALU.not_equal, fill=1.0, base=0,
                               pattern=[[-1, P]], channel_multiplier=1).then_inc(idr.sem, 1)
            for k, v in ((2, conv_ln_b), (3, gmlp_ln_g), (4, gmlp_ln_b)):
                pool.dma_start(vec_rows(k), v.rearrange("l (r c) -> (l r) c", c=P)).then_inc(ln_vec_landed.sem, 16)
            pool.dma_start(ws_nat, gmlp_ws.rearrange("l h t s -> t (l h) s")).then_inc(ws_landed.sem, 16)
            weight_lo(0, -KV)
            weight_lo(0, 1 - KV)
            pool.wait_ge(ws_landed.sem, 16)
            pool.affine_select(out=ws_low, in_=ws_nat, compare_op=ALU.is_ge, fill=0.0, base=0,
                               pattern=[[0, NH], [-1, P]], channel_multiplier=1).then_inc(msk.sem, 1)
            weight_lo(0, 2 - KV)
            pool.dma_start(bs_bc, gmlp_bs.rearrange("l h t -> (l h t)").partition_broadcast(P)).then_inc(rows_landed.sem, 16)
            for dst, v in ((bout_bc, b_out), (lng_bc, ln_g), (lnb_bc, ln_b)):
                pool.dma_start(dst[:], v.rearrange("l d -> (l d)").partition_broadcast(P)).then_inc(rows_landed.sem, 16)
            for j in range(3 - KV, WR):
                weight_lo(0, j)

            def step(b, j):
                weight_lo(b, j + WR)
                for kind, i in side.get(j - 1, []):
                    if kind == "v_turn":
                        v_norm_lo(b, i)
                    elif kind == "mix":
                        mix_gate(b, i)
                    elif kind == "score":
                        softmax_end(b, i)
                for kind, i in side.get(j, []):
                    side_stage(b, kind, i)

            def gpsimd_block(b, last):
                for j in range(OPEN, NC_IN):
                    step(b, j)
                for j in range(NC_IN, CHUNKS if not last else CHUNKS - WR):
                    weight_lo(b, j + WR)
                if last:
                    inv_std(b, LN_O)
                    for t in range(T):
                        if t < T - 1:
                            inv_std(b, LN_O + t + 1)
                            pool.wait_ge(last_scaled.sem, t + 1)
                            pool.tensor_tensor(res[:, t, :], res[:, t, :], lnb_bc[:], ALU.add).then_inc(last_added.sem, 1)
                            pool.wait_ge(last_added.sem, t + 1)
                        else:
                            pool.wait_ge(*ln_done(b, 1))
                        store(b, t)
                    return
                inv_std(b, LN_O)
                inv_std(b, LN_O + 1)
                step(b + 1, 0)
                await_rows(b, 0)
                store(b, 0)
                await_rows(b, 1)
                store(b, 1)
                step(b + 1, 1)
                step(b + 1, 2)
                inv_std(b, LN_O + 2)
                step(b + 1, 3)
                inv_std(b, LN_O + 3)
                await_rows(b, 2)
                store(b, 2)
                step(b + 1, 4)
                await_rows(b, 3)
                store(b, 3)

            for j in range(OPEN):
                step(0, j)
            with pool.Fori(0, BLOCKS - 1) as b:
                gpsimd_block(b, False)
            gpsimd_block(BLOCKS - 1, True)

        @block.vector
        def _(dve):
            def x_lo_tile(b, t):
                dve.wait_ge(*x_hi_ready(b, t + 1))
                dve.tensor_tensor(x_lo[:, :, t * P:(t + 1) * P],
                                  pair_of("x_turn", t).rearrange("p a (k s) -> p (a k) s", s=P),
                                  x_hi[:, :, t * P:(t + 1) * P].bitcast(F32),
                                  ALU.subtract).then_inc(x_split.sem, 1)

            def from_bank(b, j):
                kind, i = order[j]
                src, bias = bank_of(j), b_in_col(first[kind] + i)
                if kind == "a":
                    n, s = tmp_of[("glu", i)], i % 2
                    dve.wait_ge(*conv_summed(b, i - 1))
                    dve.wait_ge(*halo_out(b, i + 1 - NG))
                    if i > 0:
                        dve.wait_ge(*halo_out(b, i))
                    dve.tensor_copy(h[:, s, 0:PAD], halo[:, i, :]).then_inc(halo_in.sem, 1)
                    dve.wait_ge(*chunk_done(b, j + 1))
                    dve.wait_ge(*tmp_full(b, n + 1))
                    dve.scalar_tensor_tensor(h[:, s, PAD:PAD + B], src, bias, gated[:, n % 2, :],
                                             ALU.add, ALU.mult).then_inc(tmp_used.sem, 1)
                    dve.wait_ge(*tmp_used(b, n + 1))
                    dve.tensor_copy(halo[:, i, :], h[:, s, B:B + PAD]).then_inc(halo_out.sem, 1)
                elif kind == "u":
                    n = tmp_of[order[j]]
                    dve.wait_ge(*tmp_full(b, n + 1))
                    dve.wait_ge(*mix_gated(b, i + 1))
                    dve.tensor_tensor(y[:, NG + i, :], y[:, NG + i, :], gated[:, n % 2, :],
                                      ALU.mult).then_inc(tmp_used.sem, 1)
                elif kind == "conv_gate":
                    k = tmp_of[("silu", i)]
                    dve.wait_ge(*gate_ready(b, gate_of[order[j]] + 1))
                    dve.wait_ge(*tmp_full(b, k + 1))
                    dve.tensor_tensor(y[:, i, :], y[:, i, :], gated[:, k % 2, :], ALU.mult).then_inc(tmp_used.sem, 1)
                elif kind == "q":
                    dve.wait_ge(*q_hi_ready(b, i + 1))
                    dve.scalar_tensor_tensor(q_part(1, i), src, bias, q_part(0, i).bitcast(F32),
                                             ALU.add, ALU.subtract).then_inc(q_split.sem, 1)

            def tap(b, g, k):
                if k == TAPS:
                    dve.wait_ge(*tap_done(b, TAPS * (g + 1)))
                    dve.tensor_tensor(y[:, g, :], acc[1], even_sum[:], ALU.add).then_inc(conv_summed.sem, 1)
                    return
                src, w = h[:, g % 2, k:k + B], cw[:, g, k:k + 1]
                if k == 0:
                    dve.wait_ge(*tmp_used(b, tmp_of[("glu", g)] + 1))
                    dve.wait_ge(*conv_summed(b, g))
                    if g == 0:
                        dve.wait_ge(*res_summed(b, 0))
                    dve.tensor_scalar(acc[0], src, w, vec_col(CONV_B, g), ALU.mult, ALU.add).then_inc(tap_done.sem, 1)
                elif k == 1:
                    dve.tensor_scalar(acc[1], src, w, None, ALU.mult).then_inc(tap_done.sem, 1)
                else:
                    dve.wait_ge(*tap_done(b, TAPS * g + k - 1))
                    dve.scalar_tensor_tensor(even_sum[:] if k == TAPS - 1 else acc[k % 2], src, w,
                                             acc[k % 2], ALU.mult, ALU.add).then_inc(tap_done.sem, 1)

            def statistics(b, n, parts):
                for k, part in enumerate(parts):
                    dve.bn_stats(bn[:, n, k, :], part).then_inc(ln_stats.sem, 1)

            def moments(b, n):
                dve.wait_ge(*ln_stats(b, 2 * n + 2))
                dve.memset(ve[:, n:n + 1], EPS)
                dve.bn_aggr(mv[:, n, :], bn[:, n, :, :]).then_inc(ln_mean.sem, 1)
                dve.wait_ge(*ln_mean(b, n + 1))
                dve.tensor_tensor(ve[:, n:n + 1], ve[:, n:n + 1], mv[:, n, 1:2], ALU.add).then_inc(ln_var.sem, 1)

            def side_stage(b, kind, i):
                src = pair_of(kind, i)
                if kind in ("v_turn", "c_turn"):
                    n = (LN_V if kind == "v_turn" else LN_C) + i
                    dve.wait_ge(*(v_turned if kind == "v_turn" else c_turned)(b, i + 1))
                    statistics(b, n, (src[:, 0, 0:C2], src[:, 1, 0:C2]))
                    moments(b, n)
                elif kind == "mix":
                    dve.wait_ge(*mixed(b, i + 1))
                    part = mix_part(i)
                    if i >= 2:
                        dve.wait_ge(*mix_gated(b, i - 1))
                    dve.scalar_tensor_tensor(part, mix_sums(i)[:, :, 0, :], vec_col(GMLP_G, i),
                                             mix_bias[:, i:i + 1, :].to_broadcast([P, T, P]),
                                             ALU.mult, ALU.add).then_inc(mix_scaled.sem, 1)
                    dve.wait_ge(*mix_scaled(b, 2 * i + 1))
                    dve.scalar_tensor_tensor(part, mix_sums(i)[:, :, 1, :], vec_col(GMLP_G, i), part,
                                             ALU.mult, ALU.add).then_inc(mix_scaled.sem, 1)
                elif kind == "score":
                    dve.wait_ge(*scored(b, i + 1))
                    dve.tensor_reduce(mx[:, i, :], src.rearrange("p a (t m) -> p (a t) m", t=2), AX.X,
                                      ALU.max).then_inc(max_ready.sem, 1)
                    dve.wait_ge(*max_ready(b, i + 1))
                    dve.tensor_scalar(nmx[:, i, :], mx[:, i, :], -SCALE, None, ALU.mult).then_inc(nmax_ready.sem, 1)
                elif kind == "p_turn":
                    dve.wait_ge(*p_hi_ready(b, i + 1))
                    dve.tensor_tensor(p_part(1, i), src, p_part(0, i).bitcast(F32),
                                      ALU.subtract).then_inc(p_split.sem, 1)
                elif kind == "attend":
                    dve.wait_ge(*pv_done(b, i + 1))
                    dve.wait_ge(*gate_ready(b, gate_of[("x_gate", i)] + 1))
                    dve.tensor_tensor(y[:, NG + NH + i, :], src[:, 0, :], y[:, NG + NH + i, :],
                                      ALU.mult).then_inc(attended.sem, 1)
                elif kind == "c_spread":
                    dve.wait_ge(*c_spread(b, 1))
                    three = lambda n: slice(n * 3, n * 3 + 3)
                    for n in range(2):
                        dve.tensor_tensor(c_norm[:, three(n), :], y[:, three(n), :],
                                          src[:, 0:1, :].to_broadcast([P, 3, B]), ALU.subtract).then_inc(c_centred.sem, 1)
                    for n in range(2):
                        dve.wait_ge(*c_centred(b, n + 1))
                        dve.tensor_tensor(c_norm[:, three(n), :], c_norm[:, three(n), :],
                                          src[:, 1:2, :].to_broadcast([P, 3, B]), ALU.mult).then_inc(c_normed.sem, 1)

            def widen(b):
                dve.wait_ge(*ln_mean(b, LN_C + T))
                dve.tensor_copy(c_wide(0), mv[:, LN_C:LN_C + T, 0:1].to_broadcast([P, T, P])).then_inc(c_widened.sem, 1)
                dve.wait_ge(*ln_rstd(b, LN_C + T))
                dve.tensor_copy(c_wide(1), rstd[:, LN_C:LN_C + T].rearrange("p (t o) -> p t o", o=1)
                                .to_broadcast([P, T, P])).then_inc(c_widened.sem, 1)

            def inverse_sums(b, i):
                dve.wait_ge(*exp_done(b, i + 1))
                dve.reciprocal(inv[:, i, :], sums[:, i, :]).then_inc(inv_ready.sem, 1)

            def normalise(b, i):
                n = LN_V + i
                dve.wait_ge(*ln_rstd(b, n + 1))
                if i > 0:
                    dve.wait_ge(*vn_split(b, i))
                dve.tensor_scalar(v_tmp.rearrange("p (n c) -> p n c", n=2), pair_of("v_turn", i)[:, :, 0:C2],
                                  mv[:, n, 0:1], rstd[:, n:n + 1], ALU.subtract, ALU.mult).then_inc(v_normed.sem, 1)

            dve.memset(halo[:], 0.0).then_inc(halo_out.sem, 1)
            dve.memset(ones.bitcast(F32), 1.0)
            dve.wait_ge(halo_out.sem, 1)
            dve.sem_inc(halo_out.sem, NG - 1)
            dve.sem_inc(tmp_used.sem, 2)
            dve.sem_inc(conv_summed.sem, 2)
            dve.sem_inc(res_summed.sem, T)
            for i in range(MC):
                dve.wait_ge(mem_hi.sem, i + 1)
                dve.tensor_tensor(mem_part(1)[:, :, i * P:(i + 1) * P],
                                  PS[:, 2 * i:2 * i + 2, :].rearrange("p a (k s) -> p (a k) s", s=P),
                                  mem_part(0)[:, :, i * P:(i + 1) * P].bitcast(F32), ALU.subtract).then_inc(mem_split.sem, 1)
            dve.wait_ge(vec_turned.sem, 1)
            dve.tensor_copy(cw[:].rearrange("p g k -> p (g k)"), PS[:, 7, 0:NG * TAPS]).then_inc(vec_ready.sem, 1)
            dve.tensor_copy(cols[:], PS[:, 6, 0:NV]).then_inc(vec_ready.sem, 1)
            dve.wait_ge(vec_ready.sem, 2)
            for c in range(2 + T):
                if c < NX:
                    dve.wait_ge(kv_hi.sem, c + 1)
                    dve.scalar_tensor_tensor(kt[:, 1, c, :], PS[:, 4 + c % 2, 0:MEM], b_kv_col(c),
                                             kt[:, 0, c, :].bitcast(F32), ALU.add, ALU.subtract).then_inc(k_split.sem, 1)
                if c == 1:
                    dve.wait_ge(ws_hi.sem, 1)
                    dve.tensor_tensor(wst[:, 1, :, :].rearrange("p (n h) s -> p n (h s)", n=2), PS[:, 6:8, 0:C2],
                                      wst[:, 0, :, :].rearrange("p (n h) s -> p n (h s)", n=2).bitcast(F32),
                                      ALU.subtract).then_inc(ws_split.sem, 1)
                elif c >= 2:
                    x_lo_tile(0, c - 2)
            dve.wait_ge(row_sum.sem, 1)
            dve.wait_ge(rows_landed.sem, 4 * 16)
            for hd in range(NH):
                dve.scalar_tensor_tensor(mix_bias[:, hd, :], PS[:, 6 + hd // 3, hd % 3 * P:(hd % 3 + 1) * P],
                                         vec_col(GMLP_BETA, hd), bs_bc[:, hd * P:(hd + 1) * P],
                                         ALU.mult, ALU.add).then_inc(bias_ready.sem, 1)
            dve.wait_ge(v_hi.sem, 1)
            dve.tensor_tensor(vm[:, 1, :, :], PS[:, 0:2, :], vm[:, 0, :, :].bitcast(F32),
                              ALU.subtract).then_inc(v_split.sem, 1)
            dve.wait_ge(bias_ready.sem, NH)

            def y_lo(b, e):
                dve.wait_ge(*y_hi_ready(b, e + 1))
                dve.tensor_tensor(y_part(1, e), y[:, y_order[e], :], y_part(0, e).bitcast(F32),
                                  ALU.subtract).then_inc(y_split.sem, 1)

            def out_statistics(b, t):
                dve.wait_ge(*res_summed(b, t + 1))
                statistics(b, LN_O + t, (res[:, t, 0:HALF], res[:, t, HALF:D]))
                moments(b, LN_O + t)
                dve.scalar_tensor_tensor(res[:, t, :], res[:, t, :], mv[:, LN_O + t, 0:1], lng_bc[:],
                                         ALU.subtract, ALU.mult).then_inc(ln_scaled.sem, 1)

            def out_normalise(b, t):
                dve.wait_ge(*ln_scaled(b, t + 1))
                dve.wait_ge(*ln_rstd(b, LN_O + t + 1))
                dve.scalar_tensor_tensor(res[:, t, :], res[:, t, :], rstd[:, LN_O + t:LN_O + t + 1],
                                         lnb_bc[:], ALU.mult, ALU.add).then_inc(ln_done.sem, 1)

            def step(b, j, behind=None):
                from_bank(b, j)
                taps = tap_plan.get(j, [])
                for g, k in taps[:2]:
                    tap(b, g, k)
                for kind, i in side.get(j, []):
                    side_stage(b, kind, i)
                if behind:
                    out_statistics(*behind)
                for g, k in taps[2:]:
                    tap(b, g, k)
                for kind, i in side.get(j, []):
                    if kind == "v_turn":
                        normalise(b, i)
                    elif kind == "c_turn" and i == T - 1:
                        widen(b)
                    elif kind == "score":
                        inverse_sums(b, i)
                if behind:
                    out_normalise(*behind)
                if j in y_at:
                    y_lo(b, y_at[j])

            def sum_rows(b, t):
                if t < T - 1:
                    dve.wait_ge(*out_ready(b, t + 1))
                else:
                    dve.wait_ge(*chunk_done(b, CHUNKS))
                dve.wait_ge(*res_scaled(b, t + 1))
                dve.tensor_tensor(res[:, t, :], PS[:, 2 * t:2 * t + 2, :].rearrange("p a s -> p (a s)"),
                                  res[:, t, :], ALU.add).then_inc(res_summed.sem, 1)

            def vector_block(b, last):
                for j in range(OPEN, NC_IN):
                    step(b, j)
                for e in range(YR, NC_OUT):
                    y_lo(b, e)
                    if e < YR + T:
                        t = e - YR
                        dve.wait_ge(*res_landed[t](b, 1))
                        dve.scalar_tensor_tensor(res[:, t, :], res[:, t, :], ALPHA, bout_bc[:],
                                                 ALU.mult, ALU.add).then_inc(res_scaled.sem, 1)
                if last:
                    for t in range(T):
                        sum_rows(b, t)
                        out_statistics(b, t)
                    out_normalise(b, T - 1)
                    return
                sum_rows(b, 0)
                sum_rows(b, 1)
                x_lo_tile(b + 1, 0)
                sum_rows(b, 2)
                x_lo_tile(b + 1, 1)
                x_lo_tile(b + 1, 2)
                x_lo_tile(b + 1, 3)
                sum_rows(b, 3)
                for t in range(2):
                    out_statistics(b, t)
                    out_normalise(b, t)
                step(b + 1, 0)
                step(b + 1, 1)
                step(b + 1, 2, (b, 2))
                step(b + 1, 3, (b, 3))
                step(b + 1, 4)

            for j in range(OPEN):
                step(0, j)
            with dve.Fori(0, BLOCKS - 1) as b:
                vector_block(b, False)
            vector_block(BLOCKS - 1, True)


_INS = ["x", "mem", "w_in", "b_in", "conv_w", "conv_b", "conv_ln_g", "conv_ln_b", "gmlp_ln_g",
        "gmlp_ln_b", "gmlp_ws", "gmlp_bs", "w_kv", "b_kv", "w_out", "b_out", "ln_g", "ln_b"]


def kernel(**inputs):
    import numpy as np
    import concourse.bacc as bacc
    from concourse.bass_utils import run_bass_kernel_spmd

    nc = bacc.Bacc("TRN2", target_bir_lowering=False, num_devices=1)
    arrays, args = {}, []
    for name in _INS:
        a = np.ascontiguousarray(inputs[name])
        arrays[f"in_{name}"] = a
        args.append(nc.dram_tensor(f"in_{name}", a.shape, mybir.dt.from_np(a.dtype), kind="ExternalInput").ap())
    shape = arrays["in_x"].shape
    out = nc.dram_tensor("out_y", shape, F32, kind="ExternalOutput").ap()
    layer(nc, *args, out)
    r = run_bass_kernel_spmd(nc, [arrays], core_ids=[0])
    return r.results[0]["out_y"]
```
